# Optimizing a Trainium2 kernel written in Bass

```python
import jax, jax.numpy as jnp
from jax import lax
import numpy as np

D_MODEL = 1024
BATCH = 1
SEQ = 128
DEPTH = 1
DEC_BATCH = 1
DEC_SEQ = 1024
PAST_LEN = 256

GRID_W = 64
GLA_HEADS = 4
GLA_DV = (D_MODEL // 2) // GLA_HEADS
GLA_DK = GLA_DV // 2
GLA_GATE_RANK = 16
GLA_GATE_NORM = 16.0
GLA_CHUNK = 64
HEAD_DIM = 64
ATT_HEADS = (D_MODEL // 2) // HEAD_DIM
KV_HEADS = ATT_HEADS // 4
Q_BLOCK = 128
ROPE_THETA = 10000.0
ROPE_AXIS_PAIRS = HEAD_DIM // 4
N_EXPERTS = 32
TOP_K = 4
EXPERT_FF = D_MODEL
SWIGLU_LIMIT = 7.0
SWIGLU_ALPHA = 1.702
RMS_EPS = 1e-6

SPLIT_SIZES = (GLA_HEADS * GLA_DK, GLA_HEADS * GLA_DK, GLA_HEADS * GLA_DV, GLA_HEADS * GLA_DV,
               GLA_GATE_RANK, GLA_GATE_RANK,
               ATT_HEADS * HEAD_DIM, KV_HEADS * HEAD_DIM, KV_HEADS * HEAD_DIM)
D_IN = sum(SPLIT_SIZES)
D_MIX = GLA_HEADS * GLA_DV + ATT_HEADS * HEAD_DIM

kernel_name = "hybrid_gla_gqa_moe_diffusion_step"

def rms_norm(x, g):
    xf = x.astype(jnp.float32)
    y = xf * lax.rsqrt(jnp.mean(xf * xf, axis=-1, keepdims=True) + RMS_EPS)
    return (y * g.astype(jnp.float32)).astype(x.dtype)

def axial_rope(n_tok):
    rows = n_tok // GRID_W
    r, col = jnp.meshgrid(jnp.arange(rows), jnp.arange(GRID_W), indexing='ij')
    r = r.reshape(-1).astype(jnp.float32)
    col = col.reshape(-1).astype(jnp.float32)
    inv = 1.0 / (ROPE_THETA ** (jnp.arange(ROPE_AXIS_PAIRS, dtype=jnp.float32) / ROPE_AXIS_PAIRS))
    ang = jnp.concatenate([r[:, None] * inv, col[:, None] * inv], axis=-1)
    return jnp.cos(ang), jnp.sin(ang)

def apply_rope(x, cos, sin):
    xf = x.astype(jnp.float32).reshape(*x.shape[:-1], HEAD_DIM // 2, 2)
    x1, x2 = xf[..., 0], xf[..., 1]
    c = cos[None, :, None, :]
    s = sin[None, :, None, :]
    out = jnp.stack([x1 * c - x2 * s, x1 * s + x2 * c], axis=-1)
    return out.reshape(x.shape).astype(x.dtype)

def gla_chunked(q, k, v, log_a, s0):
    b_, h_, L, _ = q.shape
    n = L // GLA_CHUNK

    def chunks(t):
        return jnp.moveaxis(t.reshape(b_, h_, n, GLA_CHUNK, t.shape[-1]), 2, 0)

    lower = jnp.tril(jnp.ones((GLA_CHUNK, GLA_CHUNK), dtype=bool))[:, :, None]

    def step(S, xs):
        qc, kc, vc, gc = xs
        cum = jnp.cumsum(gc, axis=2)
        o_inter = jnp.einsum('bhik,bhkv->bhiv', qc * jnp.exp(cum), S)
        rel = jnp.exp(jnp.where(lower, cum[:, :, :, None, :] - cum[:, :, None, :, :], -jnp.inf))
        scores = jnp.einsum('bhik,bhjk,bhijk->bhij', qc, kc, rel)
        o_intra = jnp.einsum('bhij,bhjv->bhiv', scores, vc)
        last = cum[:, :, -1:, :]
        S = (jnp.exp(last[:, :, 0, :])[..., None] * S
             + jnp.einsum('bhjk,bhjv->bhkv', kc * jnp.exp(last - cum), vc))
        return S, o_inter + o_intra

    s_fin, o = lax.scan(step, s0, (chunks(q), chunks(k), chunks(v), chunks(log_a)))
    o = jnp.moveaxis(o, 0, 2).reshape(b_, h_, L, v.shape[-1])
    return o, s_fin

def block_attention(q, k, v):
    B, Sq, H, D = q.shape
    kvh = k.shape[2]
    g = H // kvh
    nq = Sq // Q_BLOCK
    qb = jnp.moveaxis(q.reshape(B, nq, Q_BLOCK, kvh, g, D), 1, 0)
    scale = HEAD_DIM ** -0.5

    def one(qblk):
        s = jnp.einsum('bqkgd,bskd->bkgqs', qblk, k, preferred_element_type=jnp.float32) * scale
        p = jax.nn.softmax(s, axis=-1).astype(v.dtype)
        return jnp.einsum('bkgqs,bskd->bqkgd', p, v)

    o = lax.map(one, qb)
    return jnp.moveaxis(o, 0, 1).reshape(B, Sq, H * D)

def token_mixer(h, w_in, w_gate_f, b_gate_f, w_gate_b, b_gate_b, gla_norm, q_norm, k_norm, w_out,
                rope, ctx_k, ctx_v, s0_f, s0_b):
    B, S, _ = h.shape
    proj = h @ w_in
    qa, ka, va, ga, lr_f, lr_b, qb, kb, vb = jnp.split(
        proj, np.cumsum(SPLIT_SIZES)[:-1].tolist(), axis=-1)

    def heads(t, n):
        return t.reshape(B, S, n, -1).transpose(0, 2, 1, 3).astype(jnp.float32)

    qa = heads(qa, GLA_HEADS) * (GLA_DK ** -0.5)
    ka = heads(ka, GLA_HEADS)
    va = heads(va, GLA_HEADS)
    la_f = heads(jax.nn.log_sigmoid((lr_f @ w_gate_f + b_gate_f).astype(jnp.float32)) / GLA_GATE_NORM, GLA_HEADS)
    la_b = heads(jax.nn.log_sigmoid((lr_b @ w_gate_b + b_gate_b).astype(jnp.float32)) / GLA_GATE_NORM, GLA_HEADS)
    o_f, s_f = gla_chunked(qa, ka, va, la_f, s0_f)
    o_r, s_b = gla_chunked(qa[:, :, ::-1], ka[:, :, ::-1], va[:, :, ::-1], la_b[:, :, ::-1], s0_b)
    o_gla = (o_f + o_r[:, :, ::-1]).transpose(0, 2, 1, 3)
    o_gla = rms_norm(o_gla, gla_norm) * jax.nn.silu(ga.reshape(B, S, GLA_HEADS, GLA_DV).astype(jnp.float32))
    o_gla = o_gla.reshape(B, S, GLA_HEADS * GLA_DV).astype(h.dtype)

    qh = rms_norm(qb.reshape(B, S, ATT_HEADS, HEAD_DIM), q_norm)
    kh = rms_norm(kb.reshape(B, S, KV_HEADS, HEAD_DIM), k_norm)
    vh = vb.reshape(B, S, KV_HEADS, HEAD_DIM)
    if rope is None:
        o_att = block_attention(qh, kh, vh)
    else:
        cos, sin = rope
        keys = jnp.concatenate([apply_rope(kh, cos, sin), ctx_k.astype(kh.dtype)], axis=1)
        vals = jnp.concatenate([vh, ctx_v.astype(vh.dtype)], axis=1)
        o_att = block_attention(apply_rope(qh, cos, sin), keys, vals)

    out = jnp.concatenate([o_gla, o_att.astype(h.dtype)], axis=-1) @ w_out
    return out, kh, vh, s_f, s_b

def moe_ffn(h, w_router, b_router, w_gu, b_gu, w_down, b_down):
    B, S, D = h.shape
    tok = h.reshape(-1, D)
    n_tok = tok.shape[0]
    logits = (tok @ w_router + b_router).astype(jnp.float32)
    top_logit, top_e = lax.top_k(logits, TOP_K)
    gate_w = jax.nn.softmax(top_logit, axis=-1)
    flat_e = top_e.reshape(-1)
    order = jnp.argsort(flat_e)
    e_sorted = flat_e[order]
    src = order // TOP_K
    group_sizes = jnp.bincount(flat_e, length=N_EXPERTS).astype(jnp.int32)
    xs = tok[src]
    gu = lax.ragged_dot(xs, w_gu, group_sizes) + b_gu[e_sorted]
    g, u = gu[:, :EXPERT_FF], gu[:, EXPERT_FF:]
    g = jnp.minimum(g, SWIGLU_LIMIT)
    u = jnp.clip(u, -SWIGLU_LIMIT, SWIGLU_LIMIT)
    act = (u + 1) * (g * jax.nn.sigmoid(SWIGLU_ALPHA * g))
    out = lax.ragged_dot(act, w_down, group_sizes) + b_down[e_sorted]
    out = out * gate_w.reshape(-1)[order][:, None].astype(out.dtype)
    y = jax.ops.segment_sum(out, src, num_segments=n_tok)
    return y.reshape(B, S, D)

def trunk_layer(x, cond, w_ada, b_ada, norm_mix, mix_p, norm_ffn, ffn_p, rope, ctx_k, ctx_v, s0_f, s0_b):
    m = (jax.nn.silu(cond) @ w_ada + b_ada)[:, None, :]
    sh1, sc1, g1, sh2, sc2, g2 = jnp.split(m, 6, axis=-1)
    h = rms_norm(x, norm_mix) * (1 + sc1) + sh1
    mo, k_c, v_c, s_f, s_b = token_mixer(h, *mix_p, rope, ctx_k, ctx_v, s0_f, s0_b)
    x = x + g1 * mo
    h = rms_norm(x, norm_ffn) * (1 + sc2) + sh2
    x = x + g2 * moe_ffn(h, *ffn_p)
    return x, k_c, v_c, s_f, s_b

def setup_inputs(seed: int = 0) -> dict:
    key = jax.random.key(seed)
    ks = jax.random.split(key, 32)

    def nrm(k, shape, s):
        return jax.random.normal(k, shape, jnp.float32) * s

    def gain(k, shape):
        return 1.0 + 0.02 * jax.random.normal(k, shape, jnp.float32)

    return {
        'x_prompt': nrm(ks[0], (BATCH, SEQ, D_MODEL), 1.0),
        'x_sample': nrm(ks[1], (DEC_BATCH, DEC_SEQ, D_MODEL), 1.0),
        'c': nrm(ks[2], (DEC_BATCH, D_MODEL), 1.0),
        'cache_k': nrm(ks[3], (DEC_BATCH, DEPTH, PAST_LEN, KV_HEADS, HEAD_DIM), 1.0),
        'cache_v': nrm(ks[4], (DEC_BATCH, DEPTH, PAST_LEN, KV_HEADS, HEAD_DIM), 1.0),
        'state_gla_fwd': nrm(ks[5], (DEC_BATCH, DEPTH, GLA_HEADS, GLA_DK, GLA_DV), 0.5),
        'state_gla_bwd': nrm(ks[6], (DEC_BATCH, DEPTH, GLA_HEADS, GLA_DK, GLA_DV), 0.5),
        'c_ctx': nrm(ks[7], (D_MODEL,), 1.0),
        'w_ada': nrm(ks[8], (DEPTH, D_MODEL, 6 * D_MODEL), D_MODEL ** -0.5),
        'b_ada': nrm(ks[9], (DEPTH, 6 * D_MODEL), 0.02),
        'norm_mix': gain(ks[10], (DEPTH, D_MODEL)),
        'w_in': nrm(ks[11], (DEPTH, D_MODEL, D_IN), D_MODEL ** -0.5),
        'w_gate_f': nrm(ks[12], (DEPTH, GLA_GATE_RANK, GLA_HEADS * GLA_DK), GLA_GATE_RANK ** -0.5),
        'b_gate_f': nrm(ks[13], (DEPTH, GLA_HEADS * GLA_DK), 0.1),
        'w_gate_b': nrm(ks[14], (DEPTH, GLA_GATE_RANK, GLA_HEADS * GLA_DK), GLA_GATE_RANK ** -0.5),
        'b_gate_b': nrm(ks[15], (DEPTH, GLA_HEADS * GLA_DK), 0.1),
        'gla_norm': gain(ks[16], (DEPTH, GLA_DV)),
        'q_norm': gain(ks[17], (DEPTH, HEAD_DIM)),
        'k_norm': gain(ks[18], (DEPTH, HEAD_DIM)),
        'w_out': nrm(ks[19], (DEPTH, D_MIX, D_MODEL), D_MIX ** -0.5),
        'norm_ffn': gain(ks[20], (DEPTH, D_MODEL)),
        'w_router': nrm(ks[21], (DEPTH, D_MODEL, N_EXPERTS), D_MODEL ** -0.5),
        'b_router': nrm(ks[22], (DEPTH, N_EXPERTS), 0.01),
        'w_gu': nrm(ks[23], (DEPTH, N_EXPERTS, D_MODEL, 2 * EXPERT_FF), D_MODEL ** -0.5),
        'b_gu': nrm(ks[24], (DEPTH, N_EXPERTS, 2 * EXPERT_FF), 0.01),
        'w_down': nrm(ks[25], (DEPTH, N_EXPERTS, EXPERT_FF, D_MODEL), EXPERT_FF ** -0.5),
        'b_down': nrm(ks[26], (DEPTH, N_EXPERTS, D_MODEL), 0.01),
        'final_norm': gain(ks[27], (D_MODEL,)),
    }

def reference(x_prompt, x_sample, c, cache_k, cache_v, state_gla_fwd, state_gla_bwd, c_ctx,
              w_ada, b_ada, norm_mix, w_in, w_gate_f, b_gate_f, w_gate_b, b_gate_b, gla_norm,
              q_norm, k_norm, w_out, norm_ffn, w_router, b_router, w_gu, b_gu, w_down, b_down,
              final_norm):
    bp = x_prompt.shape[0]
    zero_state = jnp.zeros((bp, GLA_HEADS, GLA_DK, GLA_DV), jnp.float32)
    cond_ctx = jnp.broadcast_to(c_ctx, (bp, D_MODEL))
    rope = axial_rope(x_sample.shape[1])

    xp, xs = x_prompt, x_sample
    new_k, new_v, new_sf, new_sb = [], [], [], []
    for l in range(DEPTH):
        mix_p = (w_in[l], w_gate_f[l], b_gate_f[l], w_gate_b[l], b_gate_b[l], gla_norm[l],
                 q_norm[l], k_norm[l], w_out[l])
        ffn_p = (w_router[l], b_router[l], w_gu[l], b_gu[l], w_down[l], b_down[l])
        xp, k_l, v_l, sf_l, sb_l = trunk_layer(xp, cond_ctx, w_ada[l], b_ada[l], norm_mix[l], mix_p,
                                               norm_ffn[l], ffn_p, None, None, None,
                                               zero_state, zero_state)
        new_k.append(k_l)
        new_v.append(v_l)
        new_sf.append(sf_l)
        new_sb.append(sb_l)
        xs, _, _, _, _ = trunk_layer(xs, c, w_ada[l], b_ada[l], norm_mix[l], mix_p, norm_ffn[l], ffn_p,
                                     rope, cache_k[:, l], cache_v[:, l],
                                     state_gla_fwd[:, l].astype(jnp.float32),
                                     state_gla_bwd[:, l].astype(jnp.float32))

    y_prompt = rms_norm(xp, final_norm)
    y_sample = rms_norm(xs, final_norm)
    new_cache_k = jnp.stack(new_k, axis=1).astype(x_prompt.dtype)
    new_cache_v = jnp.stack(new_v, axis=1).astype(x_prompt.dtype)
    new_state_gla_fwd = jnp.stack(new_sf, axis=1).astype(x_prompt.dtype)
    new_state_gla_bwd = jnp.stack(new_sb, axis=1).astype(x_prompt.dtype)
    return (y_prompt, y_sample, new_cache_k, new_cache_v, new_state_gla_fwd, new_state_gla_bwd)


_drawn_inputs = setup_inputs


def setup_inputs(seed=0):
    import zlib

    import numpy as np

    out = dict(_drawn_inputs(seed))
    spreads = {}
    factors = {'state_gla_fwd': 44.27,
     'state_gla_bwd': 39.358,
     'gla_norm': 2.672,
     'q_norm': 8.0,
     'k_norm': 2.814,
     'b_gu': 8.0,
     'b_down': 25.321,
     'final_norm': 30.671,
     'cache_k': 8.0,
     'cache_v': 8.0,
     'b_router': 3.139}
    for name, (base, spread) in spreads.items():
        noise = np.random.default_rng([zlib.crc32(name.encode()), seed]).standard_normal(out[name].shape)
        drawn = base * np.exp(spread * noise) if base else spread * noise
        out[name] = __import__('jax').numpy.asarray(drawn.astype(out[name].dtype))
    for name, factor in factors.items():
        out[name] = (out[name] * factor).astype(out[name].dtype)
    return out
```

```python
import concourse.bass as bass
from concourse import mybir
from contextlib import ExitStack, contextmanager

P = 128


class Chain:

    def __init__(self, eng, sem):
        self.eng, self.sem, self.base, self.n = eng, sem, 0, 0

    def start(self, base=0):
        self.base, self.n = base, 0

    def link(self, ins):
        ins.then_inc(self.sem, 1)
        self.n += 1
        self.eng.wait_ge(self.sem, self.base + self.n)


def trunk_kernel(nc, t_in, t_out):
    F32, I32, U32 = mybir.dt.float32, mybir.dt.int32, mybir.dt.uint32
    ALU, ACT, AX = mybir.AluOpType, mybir.ActivationFunctionType, mybir.AxisListType
    ds = bass.ds

    DM = t_in["x_sample"].shape[2]
    KT = DM // P
    NS = t_in["x_sample"].shape[1] // P
    NT = NS + 1
    TOK = NT * P
    DIN = t_in["w_in"].shape[2]
    HD = t_in["q_norm"].shape[1]
    NH, GH, DV = 8, 4, P
    NKV = t_in["cache_k"].shape[3]
    NC = t_in["cache_k"].shape[2] // P
    RANK = t_in["w_gate_f"].shape[1]
    NE = t_in["w_router"].shape[2]
    TOPK = 4
    FF = t_in["w_down"].shape[2]
    EPS = 1e-6
    H = 512
    KEYS = (NS + NC) * P
    C_LR, C_QB, C_KB = 1536, 1568, 2080
    LISTW = TOK
    PADS = P
    CHUNKS = 6

    hid = lambda name, shape, dt=F32: nc.dram_tensor(name, shape, dt, kind="Internal").ap()
    mod_d = hid("mod_rows", (2, 6, DM))
    x1_d = hid("x_after_mixing", (TOK, DM))
    h2_d = hid("expert_inputs", (TOK + PADS, DM))
    moe_d = hid("expert_sums", (TOK + PADS, DM))
    list_d = hid("expert_lists", (NE * LISTW, 2), I32)

    x_lat = t_in["x_sample"][0]
    x_ctx = t_in["x_prompt"][0]
    w_in_v = t_in["w_in"][0].rearrange("(j p) n -> p j n", p=P)
    w_out_v = t_in["w_out"][0].rearrange("(j p) n -> p j n", p=P)
    w_ada_v = t_in["w_ada"][0].rearrange("(j p) n -> p j n", p=P)
    w_rt_v = t_in["w_router"][0].rearrange("(j p) n -> p j n", p=P)

    def spread(row, n=P):
        return row.rearrange("(o n) -> o n", o=1).broadcast_to([n, row.shape[0]])

    ctx = ExitStack()
    with ctx:
        W = 53200
        AR = ctx.enter_context(nc.sbuf_tensor("arena", [P, W], F32))
        PS = ctx.enter_context(nc.psum_tensor("psum", [P, 8 * H], F32))
        sems = {}

        def sem(name):
            if name not in sems:
                sems[name] = nc.alloc_semaphore(name=name)
            return sems[name]

        @contextmanager
        def stage(keep):
            with nc.Block() as block:
                yield block
            done = [n for n in sems if n not in keep.split() + ["ident_in"]]
            with nc.Block() as clear:
                @clear.sync
                def _(sp):
                    for n in done:
                        sp.sem_clear(sems[n])
            for n in done:
                nc.release_semaphore(sems.pop(n))

        def ar(at, n, rows=P, r0=0):
            assert at + n <= W
            return AR[r0:r0 + rows, at:at + n]

        def r3(ap, a):
            return ap.rearrange("p (a b) -> p a b", a=a)

        qkT = r3(ar(0, 4 * TOK), 4)
        v_all = r3(ar(4608, NT * H), NT)
        ga_all = r3(ar(9216, NT * H), NT)
        qaT = r3(ar(13824, 4 * TOK), 4)
        kaT = ar(18432, TOK + NC * P)
        va = r3(ar(19840, (NT + NC) * P), NT + NC)
        lrT = ar(21248, TOK, 2 * RANK)
        w_in = r3(ar(22400, KT * DIN), KT)
        xs = [ar(41088 + DM * i, DM) for i in range(2)]
        hT = [ar(43136 + DM * i, DM) for i in range(2)]
        mA = [ar(45184, DM), ar(46208, DM)]
        mAc = [ar(21248, DM), ar(44160, DM)]
        xjunk = ar(47232, H).bitcast(mybir.dt.bfloat16)
        sq = ar(47744, 640)
        qks = ar(48384, 512)
        sg = ar(48896, 512)
        qn = ar(49408, 640)
        qw = ar(50048, 640)
        qr = ar(50688, 640)
        lrs = ar(51328, 32)
        rope = [ar(51360 + 128 * i, 128) for i in range(2)]
        ident = ar(51616, P)
        nw = ar(51744, 2 * HD)
        gn = ar(51872, DV)
        small = ar(52000, 680)
        so = [0]

        def sm(n, rows=P):
            so[0] += n
            return small[0:rows, so[0] - n:so[0]]

        RING_A = [r3(ar(4608 + 4096 * i, 4096), KT) for i in range(3)]
        crow = ar(0, P, 2 * KT)
        scT = ar(52936, 2 * KT)
        sgc = ar(144, 2 * KT)
        brow = ar(512, 2048, 2)
        mrow = ar(2560, 2048, 2)
        nrow = ar(16896, DM, 2)
        D = ar(22400, 4 * TOK).rearrange("p (d q t) -> p d q t", d=2, q=2)
        RING_B = [r3(ar(27008 + 4096 * i, 4096), KT) for i in range(3)]
        ab = [ar(41088 + TOK * i, TOK) for i in range(2)]
        lg = [ar(43392 + TOK * i, TOK) for i in range(2)]
        pre = ar(45696, TOK)
        keep = ar(46848, TOK)
        brow2 = [ar(48000 + 1536 * i, H, 2) for i in range(2)]
        mrow2 = [ar(48512 + 1536 * i, H, 2) for i in range(2)]
        nrow2 = [ar(49024 + 1536 * i, H, 2) for i in range(2)]
        ek = ar(41088, H)
        kf = ar(41600, H)
        kTM = ar(42112, H)
        U = ar(42624, NT * H).rearrange("p (g u c) -> p g u c", g=NT, u=4)
        S = r3(ar(36224, H), 4)
        St = r3(ar(36736, H), 4)
        seen = ar(37248, H).bitcast(I32)
        Sb = ar(27008, NT * 2 * H).rearrange("p (g u h c) -> p g u h c", g=NT, u=4, h=2)
        eq = ar(41088, H)
        ekc = ar(41600, H)
        qf = ar(42112, H)
        kfc = ar(42624, H)
        sc = [ar(43136 + H * i, H) for i in range(2)]
        osq = ar(44160, H)
        on = ar(44672, H)
        oatt = r3(ar(36224, NT * H), NT)
        qst = ar(45184, H)
        pr = [ar(45696 + KEYS * i, KEYS) for i in range(2)]
        pT = [ar(48256 + KEYS * i, KEYS) for i in range(2)]
        kc = r3(ar(50816, NC * P), NC)
        w_out = r3(ar(27008, KT * DM), KT)
        mE = [[ar(3 * DM * c + DM * i, DM) for i in range(3)] for c in range(2)]
        xr = ar(41472, DM)
        mixs = ar(42496, DM)
        x1 = ar(43520, DM)
        h2 = ar(44544, DM)
        mixT = ar(45568, DM)
        h2T = ar(46592, DM)
        junkE = ar(47616, H).bitcast(mybir.dt.bfloat16)
        w_rt = r3(ar(48128, KT * NE), KT)
        zeros = ar(49984, DM)
        spares = r3(ar(51072, TOPK * NE), TOPK)
        wc = [ar(13824 + 4096 * i, 4096) for i in range(CHUNKS)]
        bias = ar(38400, 3 * DM)
        xg, xT, gw, uw, act, actT, yo = (ar(DM * i, DM) for i in range(7))
        sgm = ar(7 * DM, H)
        ys = [ar(DM * i, DM) for i in range(2)]
        xf = [ar(2 * DM + DM * i, DM) for i in range(2)]
        mG = [ar(4 * DM, DM), ar(5 * DM, DM)]
        fn = ar(6 * DM, DM)
        yf = [ar(7 * DM + DM * i, DM) for i in range(2)]

        WG = ar(51072, 2 * 2 * P, 2 * RANK).rearrange("p (d c) -> p d c", d=2)

        upper = ar(52680, P)
        ones = ar(52808, P)
        negh = sm(10)
        ss, msq, rstd = sm(1), sm(1), sm(1)
        ssq, vq, rq = sm(10), sm(10), sm(10)
        so4, vo4, ro4 = sm(4), sm(4), sm(4)
        vecs = sm(3 * 4 * NT).rearrange("p (k u g) -> p k u g", k=3, u=4)
        bgate = sm(4)
        mx, nmx, rs, rrs = sm(8), sm(8), sm(8), sm(8)
        top8, idxf, exg, gates = sm(8), sm(8), sm(4), sm(4)
        top8i = sm(8).bitcast(U32)
        gsum, gcp, ntop = sm(1), sm(1), sm(1)
        slotf, sloti = sm(4), sm(4).bitcast(I32)
        ent = sm(8).bitcast(I32)
        logit, brt, picked, pickedsum, place, expert, spare = (sm(NE) for _ in range(7))
        tokid = sm(NT)
        cnti, ntl, tstartf = sm(NE).bitcast(I32), sm(NE), sm(NE)
        tstart = sm(NE + 1).bitcast(I32)
        listed, current = sm(2).bitcast(I32), sm(2)

        def bank(b, n=H, off=0):
            return PS[:, b * H + off:b * H + off + n]

        def bc(ap, n):
            p_, a_ = ap.shape
            return ap.unsqueeze(2).broadcast_to([p_, a_, n])

        def wait(eng, sem_, value):
            eng.wait_ge(sem_, value)
            if not isinstance(value, int):
                eng.wait_ge(sem("ident_in"), 16)

        def settle(eng, steps):
            eng.sem_inc(sem(steps), 1)

        with stage("const_set norms_in pads_out modc_in modl_in w_in_in x_in0 x_in1 rope_in1") as block:
            @block.sync
            def _(sp):
                sp.dma_start(crow[0:KT, :], t_in["c"][0].rearrange("(j p) -> j p", p=P)).then_inc(sem("cond_in"), 16)
                sp.dma_start(crow[KT:2 * KT, :], t_in["c_ctx"].rearrange("(j p) -> j p", p=P)).then_inc(sem("cond_in"), 16)
                sp.dma_start(ident, t_in["ident"]).then_inc(sem("ident_in"), 16)
                for n in range(4):
                    if n >= 3:
                        sp.wait_ge(sem("ada1_made"), n - 2)
                    sp.dma_start(RING_A[n % 3], w_ada_v[:, :, n * H:(n + 1) * H]).then_inc(sem(f"ada_in{n}"), 16)
                for j in range(KT):
                    sp.dma_start(w_in[:, j, :], w_in_v[:, j, :]).then_inc(sem("w_in_in"), 16)
                sp.wait_ge(sem("mod1_ready"), 4)
                sp.dma_start(mod_d[:, 0:2, :], mrow.rearrange("p (a b) -> p a b", a=2)).then_inc(sem("mod1_out"), 16)
                sp.wait_ge(sem("mod1_out"), 16)
                for i, r in ((0, 1), (1, 0)):
                    sp.dma_start(mAc[i], spread(mod_d[1, r])).then_inc(sem("modc_in"), 16)
                for i, r in ((0, 1), (1, 0)):
                    sp.dma_start(mA[i], spread(mod_d[0, r])).then_inc(sem("modl_in"), 16)

            @block.scalar
            def _(act):
                act.dma_start(brow, spread(t_in["b_ada"][0, 0:2048], 2)).then_inc(sem("brow_in"), 16)
                act.dma_start(nrow, spread(t_in["norm_mix"][0], 2)).then_inc(sem("brow_in"), 16)
                act.dma_start(xs[0], x_ctx).then_inc(sem("x_in0"), 16)
                act.dma_start(xs[1], x_lat[0:P, :]).then_inc(sem("x_in1"), 16)
                act.dma_start(rope[1], t_in["rope"][0:P, :]).then_inc(sem("rope_in1"), 16)
                act.dma_start(nw[:, 0:HD], spread(t_in["q_norm"][0])).then_inc(sem("norms_in"), 16)
                act.dma_start(nw[:, HD:2 * HD], spread(t_in["k_norm"][0])).then_inc(sem("norms_in"), 16)
                act.dma_start(gn, spread(t_in["gla_norm"][0])).then_inc(sem("norms_in"), 16)
                act.dma_start(upper, t_in["upper"]).then_inc(sem("norms_in"), 16)
                act.dma_start(tokid, t_in["tokid"]).then_inc(sem("norms_in"), 16)
                act.dma_start(expert, spread(t_in["expert_id"])).then_inc(sem("norms_in"), 16)
                act.dma_start(brt, spread(t_in["b_router"][0])).then_inc(sem("norms_in"), 16)
                act.dma_start(list_d.rearrange("(p a) w -> p (a w)", p=P), t_in["list_pads"].rearrange("(p a) w -> p (a w)", p=P)).then_inc(sem("pads_out"), 16)
                act.wait_ge(sem("condT_made"), 1)
                nc.scalar.activation(sgc, bank(7, 2 * KT), ACT.Sigmoid).then_inc(sem("cond_sig"), 1)

            @block.gpsimd
            def _(pool):
                nc.gpsimd.memset(negh, -0.5).then_inc(sem("const_set"), 1)
                nc.gpsimd.memset(ones, 1.0).then_inc(sem("const_set"), 1)
                nc.gpsimd.memset(pickedsum, 0.0).then_inc(sem("const_set"), 1)

            @block.vector
            def _(dve):
                dve.wait_ge(sem("cond_sig"), 1)
                nc.vector.tensor_tensor(scT, bank(7, 2 * KT), sgc, ALU.mult).then_inc(sem("scT_ready"), 1)
                dve.wait_ge(sem("brow_in"), 32)
                own = Chain(dve, sem("own_a0"))
                for n in range(4):
                    piece = mrow[:, n * H:(n + 1) * H]
                    dve.wait_ge(sem("ada1_made"), n + 1)
                    add = nc.vector.tensor_tensor(piece, bank(n)[0:2, :], brow[:, n * H:(n + 1) * H], ALU.add)
                    if n < 2:
                        add.then_inc(sem("mod1_ready"), 1)
                    else:
                        own.link(add)
                        nc.vector.scalar_tensor_tensor(piece, piece, 1.0, nrow[:, (n - 2) * H:(n - 1) * H],
                                                       ALU.add, ALU.mult).then_inc(sem("mod1_ready"), 1)

            @block.tensor
            def _(pe):
                pe.wait_ge(sem("cond_in"), 32)
                pe.wait_ge(sem("ident_in"), 16)
                nc.tensor.transpose(bank(7, 2 * KT), crow, ident[0:2 * KT, 0:2 * KT]).then_inc(sem("condT_made"), 1)
                pe.wait_ge(sem("scT_ready"), 1)
                for n in range(4):
                    pe.wait_ge(sem(f"ada_in{n}"), 16)
                    for j in range(KT):
                        last = nc.tensor.matmul(bank(n)[0:2, :], scT[:, j:2 * KT:KT], RING_A[n % 3][:, j, :],
                                                start=(j == 0), stop=(j == KT - 1))
                    last.then_inc(sem("ada1_made"), 1)

        with stage("const_set pads_out") as block:
            def tiles(eng, body):
                body(0, 0, 1, False)
                with eng.Fori(0, NS // 2) as i:
                    body(i * 2 + 1, 1, i + 1, True)
                    body(i * 2 + 2, 0, i + 2, True)

            @block.sync
            def _(sp):
                def load(g, slot, src_tile):
                    wait(sp, sem("x_transposed"), g - 1)
                    sp.dma_start(xs[slot], x_lat[ds(src_tile * P, P), :]).then_inc(sem(f"x_in{slot}"), 16)
                    wait(sp, sem("rotated"), g - 1)
                    sp.dma_start(rope[slot], t_in["rope"][ds(src_tile * P, P), :]).then_inc(sem(f"rope_in{slot}"), 16)

                sp.wait_ge(sem("rotated"), 1)
                sp.wait_ge(sem("va_kept"), 1)
                sp.dma_start(t_out["new_k"][0, 0].rearrange("s h d -> s (h d)"), qr[:, H:H + P]).then_inc(sem("out_kv"), 16)
                sp.dma_start(t_out["new_v"][0, 0].rearrange("s h d -> s (h d)"), va[:, 0, :]).then_inc(sem("out_kv"), 16)
                with sp.Fori(0, NS // 2 - 1) as i:
                    load(i * 2 + 2, 0, i * 2 + 1)
                    load(i * 2 + 3, 1, i * 2 + 2)
                load(NS, 0, NS - 1)
                sp.wait_ge(sem("x_transposed"), NS)
                sp.dma_start(xs[1], x_lat[0:P, :]).then_inc(sem("x_in1"), 16)

            @block.scalar
            def _(act):
                act.wait_ge(sem("x_in0"), 16)
                nc.scalar.activation(xjunk, xs[0], ACT.Square, accum_out=ss).then_inc(sem("x_squared"), 1)
                def body(g, b, n, latent):
                    nb, nn = 1 - b, (n if b == 0 else n + 1)
                    wait(act, sem(f"x_in{nb}"), nn * 16)
                    wait(act, sem("x_normed"), g + 1)
                    nc.scalar.activation(xjunk, xs[nb], ACT.Square, accum_out=ss).then_inc(sem("x_squared"), 1)
                    wait(act, sem("proj_qb"), g + 1)
                    wait(act, sem("rotated"), g)
                    nc.scalar.activation(sq[:, 0:H], bank(2), ACT.Square).then_inc(sem("qb_squared"), 1)
                    wait(act, sem("proj_kv"), g + 1)
                    wait(act, sem("lr_transposed"), g)
                    nc.scalar.activation(lrs, bank(3, 32), ACT.Copy).then_inc(sem("lr_staged"), 1)
                    nc.scalar.activation(va[:, ds(g, 1), :], bank(3, P, 32 + P).unsqueeze(1), ACT.Copy).then_inc(sem("va_kept"), 1)
                    nc.scalar.activation(sq[:, H:H + P], bank(3, P, 32), ACT.Square).then_inc(sem("kb_squared"), 1)
                    wait(act, sem("x_transposed"), g + 2)
                    wait(act, sem("proj_ga"), g)
                    nc.scalar.activation(hT[nb], PS[:, 0:DM], ACT.Copy).then_inc(sem("hT_ready"), 1)
                    wait(act, sem("proj_qk"), g + 1)
                    wait(act, sem("qk_transposed"), g)
                    nc.scalar.activation(qks, bank(4), ACT.Copy).then_inc(sem("qk_staged"), 1)
                    wait(act, sem("qk_transposed"), g + 1)
                    nc.scalar.activation(qkT[:, :, ds(g * P, P)], r3(bank(7), 4), ACT.Copy).then_inc(sem("qkT_kept"), 1)
                    wait(act, sem("proj_ga"), g + 1)
                    wait(act, sem("ga_kept"), g)
                    nc.scalar.activation(sg, bank(6), ACT.Sigmoid).then_inc(sem("ga_sig"), 1)
                    wait(act, sem("lr_transposed"), g + 1)
                    nc.scalar.activation(kaT[:, ds(g * P, P)], bank(7, P), ACT.Copy)
                    nc.scalar.activation(lrT[:, ds(g * P, P)], PS[0:32, 7 * H + P:7 * H + 2 * P], ACT.Copy).then_inc(sem("lrT_kept"), 1)

                act.wait_ge(sem("x_transposed"), 1)
                nc.scalar.activation(hT[0], PS[:, 0:DM], ACT.Copy).then_inc(sem("hT_ready"), 1)
                tiles(act, body)

            @block.gpsimd
            def _(pool):
                pool.wait_ge(sem("norms_in"), 16 * 7)
                pool.wait_ge(sem("const_set"), 3)

                def norm_x(n):
                    wait(pool, sem("x_mean"), n)
                    nc.gpsimd.tensor_tensor(rstd, msq, negh[:, 0:1], ALU.pow).then_inc(sem("x_rstd"), 1)

                norm_x(1)
                def body(g, b, n, latent):
                    norm_x(g + 2)
                    wait(pool, sem("qk_mean"), g + 1)
                    nc.gpsimd.tensor_tensor(rq, vq, negh, ALU.pow).then_inc(sem("qk_rstd"), 1)
                    wait(pool, sem("qk_scaled"), g + 1)
                    wait(pool, sem("rotated"), g)
                    for lo, m, half in ((0, NH, 0), (H, NKV, 1)):
                        nc.gpsimd.tensor_tensor(r3(qw[:, lo:lo + m * HD], m), r3(qn[:, lo:lo + m * HD], m),
                                                nw[:, half * HD:half * HD + HD].unsqueeze(1).broadcast_to([P, m, HD]),
                                                ALU.mult).then_inc(sem("qk_weighted"), 1)
                    if latent:
                        wait(pool, sem("qk_weighted"), g * 2 + 2)
                        wait(pool, sem(f"rope_in{b}"), (n if b else n - 1) * 16)
                        S2 = rope[b][:, HD:2 * HD]
                        pairs = lambda ap, o: ap.rearrange("p (h c two) -> p h c two", h=NH + NKV, two=2)[:, :, :, o]
                        for o in range(2):
                            nc.gpsimd.tensor_tensor(pairs(qn, o), pairs(qw, 1 - o),
                                                    S2.rearrange("p (c two) -> p c two", two=2)[:, :, o].unsqueeze(1)
                                                    .broadcast_to([P, NH + NKV, HD // 2]),
                                                    ALU.mult).then_inc(sem("swapped"), 1)
                    wait(pool, sem("ga_kept"), g + 1)
                    gg = ga_all[:, ds(g, 1), :].rearrange("p a (h c) -> p (a h) c", h=GH)
                    nc.gpsimd.tensor_tensor(gg, gg, gn.unsqueeze(1).broadcast_to([P, GH, DV]), ALU.mult).then_inc(sem("ga_done"), 1)

                tiles(pool, body)

            @block.vector
            def _(dve):
                own = Chain(dve, sem("own_a"))
                own.start(0)
                dve.wait_ge(sem("modc_in"), 32)
                dve.wait_ge(sem("modl_in"), 32)

                def norm_x(g, slot, nload, mods):
                    wait(dve, sem("x_squared"), g + 1)
                    nc.vector.tensor_scalar(msq, ss, 1.0 / DM, EPS, ALU.mult, ALU.add).then_inc(sem("x_mean"), 1)
                    wait(dve, sem("x_rstd"), g + 1)
                    own.link(nc.vector.scalar_tensor_tensor(xs[slot], xs[slot], rstd, mods[0], ALU.mult, ALU.mult))
                    nc.vector.tensor_tensor(xs[slot], xs[slot], mods[1], ALU.add).then_inc(sem("x_normed"), 1)

                def by_head(ap, order):
                    return ap[:, 0:H].rearrange(f"p ({order} c) -> p v r c", v=NKV, r=NH // NKV)

                norm_x(0, 0, 1, mAc)
                def body(g, b, n, latent):
                    own.start(g * 3 if latent else 1)
                    norm_x(g + 1, 1 - b, None, mA)
                    wait(dve, sem("kb_squared"), g + 1)
                    own.link(nc.vector.tensor_reduce(ssq, r3(sq, NH + NKV), AX.X, ALU.add))
                    nc.vector.tensor_scalar(vq, ssq, 1.0 / HD, EPS, ALU.mult, ALU.add).then_inc(sem("qk_mean"), 1)
                    wait(dve, sem("qk_rstd"), g + 1)
                    nc.vector.tensor_tensor(r3(qn[:, 0:H], NH), r3(bank(2), NH), bc(rq[:, 0:NH], HD), ALU.mult).then_inc(sem("q_scaled"), 1)
                    nc.vector.tensor_tensor(r3(qn[:, H:H + P], NKV), r3(bank(3, P, 32), NKV), bc(rq[:, NH:NH + NKV], HD),
                                            ALU.mult).then_inc(sem("qk_scaled"), 1)
                    if latent:
                        C2 = rope[b][:, 0:HD]
                        wait(dve, sem("qk_weighted"), g * 2 + 2)
                        wait(dve, sem(f"rope_in{b}"), (n if b else n - 1) * 16)
                        own.link(nc.vector.tensor_tensor(r3(sq, NH + NKV), r3(qw, NH + NKV),
                                                         C2.unsqueeze(1).broadcast_to([P, NH + NKV, HD]), ALU.mult))
                        wait(dve, sem("swapped"), g * 2)
                        wait(dve, sem("lr_transposed"), g)
                        dve.wait_ge(sem("out_kv"), 32)
                        nc.vector.tensor_tensor(by_head(qr, "r v"), by_head(sq, "v r"), by_head(qn, "v r"), ALU.add)
                        nc.vector.tensor_tensor(qr[:, H:H + P], sq[:, H:H + P], qn[:, H:H + P], ALU.add).then_inc(sem("rotated"), 1)
                    else:
                        dve.wait_ge(sem("qk_weighted"), 2)
                        nc.vector.tensor_copy(by_head(qr, "r v"), by_head(qw, "v r"))
                        nc.vector.tensor_copy(qr[:, H:H + P], qw[:, H:H + P]).then_inc(sem("rotated"), 1)
                    wait(dve, sem("qa_transposed"), g + 1)
                    nc.vector.tensor_copy(qaT[:, :, ds(g * P, P)], r3(bank(7), 4)).then_inc(sem("qaT_kept"), 1)
                    wait(dve, sem("proj_va"), g + 1)
                    nc.vector.tensor_copy(v_all[:, ds(g, 1), :], bank(5).unsqueeze(1)).then_inc(sem("v_kept"), 1)
                    wait(dve, sem("ga_sig"), g + 1)
                    nc.vector.tensor_tensor(ga_all[:, ds(g, 1), :], bank(6).unsqueeze(1), sg.unsqueeze(1), ALU.mult).then_inc(sem("ga_kept"), 1)

                tiles(dve, body)

            @block.tensor
            def _(pe):
                def x_transpose(g, slot):
                    wait(pe, sem("x_normed"), g + 1)
                    wait(pe, sem("hT_ready"), g)
                    for j in range(KT):
                        last = nc.tensor.transpose(PS[:, j * P:(j + 1) * P], xs[slot][:, j * P:(j + 1) * P], ident)
                    last.then_inc(sem("x_transposed"), 1)

                def project(b, bk, off, lo, n, done):
                    for j in range(KT):
                        last = nc.tensor.matmul(bank(bk, n, off), hT[b][:, j * P:(j + 1) * P], w_in[:, j, lo:lo + n],
                                                start=(j == 0), stop=(j == KT - 1))
                    if done:
                        last.then_inc(sem(done), 1)

                x_transpose(0, 0)
                pe.wait_ge(sem("w_in_in"), 16 * KT)

                def body(g, b, n, latent):
                    wait(pe, sem("hT_ready"), g + 1)
                    wait(pe, sem("qk_scaled"), g)
                    project(b, 2, 0, C_QB, H, "proj_qb")
                    project(b, 3, 0, C_LR, 32, None)
                    project(b, 3, 32, C_KB, 2 * P, "proj_kv")
                    x_transpose(g + 1, 1 - b)
                    wait(pe, sem("qk_staged"), g)
                    project(b, 4, 0, 0, H, "proj_qk")
                    wait(pe, sem("rotated"), g + 1)
                    wait(pe, sem("lrT_kept"), g)
                    for r in range(4):
                        last = nc.tensor.transpose(bank(7, P, r * P), qr[:, r * P:(r + 1) * P], ident)
                    last.then_inc(sem("qa_transposed"), 1)
                    wait(pe, sem("v_kept"), g)
                    project(b, 5, 0, 512, H, "proj_va")
                    wait(pe, sem("qk_staged"), g + 1)
                    wait(pe, sem("qaT_kept"), g + 1)
                    for r in range(4):
                        last = nc.tensor.transpose(bank(7, P, r * P), qks[:, r * P:(r + 1) * P], ident)
                    last.then_inc(sem("qk_transposed"), 1)
                    wait(pe, sem("ga_kept"), g)
                    project(b, 6, 0, 1024, H, "proj_ga")
                    wait(pe, sem("lr_staged"), g + 1)
                    wait(pe, sem("qkT_kept"), g + 1)
                    nc.tensor.transpose(bank(7, P), qr[:, H:H + P], ident)
                    nc.tensor.transpose(PS[0:32, 7 * H + P:7 * H + 2 * P], lrs, ident).then_inc(sem("lr_transposed"), 1)

                tiles(pe, body)

        NADA = 8
        with stage("pads_out state_in vecs_ready seen_in") as block:
            @block.sync
            def _(sp):
                sp.wait_ge(sem("const_set"), 4)
                sp.dma_start(WG[0:RANK, 0, :], t_in["w_gate_f"][0]).then_inc(sem("gate_w_in"), 16)
                sp.dma_start(WG[RANK:2 * RANK, 1, :], t_in["w_gate_b"][0]).then_inc(sem("gate_w_in"), 16)
                for d, name in enumerate(("b_gate_f", "b_gate_b")):
                    for q in range(2):
                        sp.dma_start(bgate[:, 2 * d + q:2 * d + q + 1],
                                     t_in[name][0, q * P:(q + 1) * P].rearrange("(p o) -> p o", o=1)).then_inc(sem("gate_b_in"), 16)
                sp.dma_start(keep, spread(t_in["keep"])).then_inc(sem("keep_in"), 16)
                for n in range(NADA):
                    if n >= 3:
                        sp.wait_ge(sem("ada2_made"), n - 2)
                    sp.dma_start(RING_B[n % 3], w_ada_v[:, :, (n + 4) * H:(n + 5) * H]).then_inc(sem(f"ada2_in{n % 3}"), 16)
                    if n >= 2:
                        sp.wait_ge(sem("mod2_ready"), n - 1)
                    sp.dma_start(brow2[n % 2], spread(t_in["b_ada"][0, (n + 4) * H:(n + 5) * H], 2)).then_inc(sem(f"brow2_in{n % 2}"), 16)
                    if n in (4, 5):
                        sp.dma_start(nrow2[n % 2], spread(t_in["norm_ffn"][0, (n - 4) * H:(n - 3) * H], 2)).then_inc(sem("nrow2_in"), 16)
                sp.wait_ge(sem("ada2_made"), NADA - 2)
                sp.dma_start(seen, t_in["seen"]).then_inc(sem("seen_in"), 16)
                for d, name in enumerate(("state_gla_fwd", "state_gla_bwd")):
                    for half in range(2):
                        sp.dma_start(S[64 * half:64 * half + 64, 2 * d:2 * d + 2, :],
                                     t_in[name][0, 0].rearrange("(q h) k v -> h k q v", h=2)[half]).then_inc(sem("state_in"), 16)

            @block.scalar
            def _(act):
                own = Chain(act, sem("own_b1_act"))
                act.wait_ge(sem("gate_b_in"), 64)
                for u in range(4):
                    z = PS[:, (u % 2) * 3 * H:(u % 2) * 3 * H + 3 * H].rearrange("p (a b) -> p a b", a=3)[:, :, 0:384]
                    a = ab[u % 2]
                    act.wait_ge(sem("z_made"), u + 1)
                    if u >= 2:
                        act.wait_ge(sem("decay_logged"), u - 1)
                    nc.scalar.activation(r3(a, 3), z, ACT.Abs, bias=bgate[:, u:u + 1]).then_inc(sem("abs_made"), 1)
                    act.wait_ge(sem("abs_made"), u + 1)
                    own.link(nc.scalar.activation(a, a, ACT.Exp, scale=-1.0))
                    nc.scalar.activation(a, a, ACT.Ln, bias=1.0).then_inc(sem("ln_made"), 1)
                act.wait_ge(sem("vecs_raw"), 4)
                flat = vecs.rearrange("p k u g -> p (k u g)")
                nc.scalar.activation(flat, flat, ACT.Exp, scale=1.0 / 16).then_inc(sem("vecs_ready"), 1)

            @block.gpsimd
            def _(pool):
                nc.gpsimd.memset(ar(51072, 2 * 2 * P, 2 * RANK), 0.0).then_inc(sem("const_set"), 1)
                for n in range(NADA):
                    pool.wait_ge(sem("mod2_ready"), n + 1)
                    pool.dma_start(mod_d[:, 2 + n // 2, (n % 2) * H:(n % 2 + 1) * H], mrow2[n % 2]).then_inc(sem(f"mod2_out{n % 2}"), 16)
                pool.wait_ge(sem("mod2_out0"), 16 * NADA // 2)
                pool.wait_ge(sem("mod2_out1"), 16 * NADA // 2)

            @block.vector
            def _(dve):
                own = Chain(dve, sem("own_b1"))
                dve.wait_ge(sem("keep_in"), 16)

                def decay(u):
                    d = u // 2
                    z = PS[:, (u % 2) * 3 * H:(u % 2) * 3 * H + 3 * H].rearrange("p (a b) -> p a b", a=3)[:, :, 0:384]
                    l = lg[u % 2]
                    dve.wait_ge(sem("abs_made"), u + 1)
                    nc.vector.tensor_scalar(r3(l, 3), z, bgate[:, u:u + 1], 0.0, ALU.add, ALU.min).then_inc(sem("z_read"), 1)
                    dve.wait_ge(sem("z_read"), u + 1)
                    dve.wait_ge(sem("ln_made"), u + 1)
                    nc.vector.tensor_tensor(l, l, ab[u % 2], ALU.subtract).then_inc(sem("decay_logged"), 1)
                    dve.wait_ge(sem("decay_logged"), u + 1)
                    own.link(nc.vector.tensor_tensor_scan(pre, keep, l, 0.0, ALU.mult, ALU.add))
                    p3, l3, D3 = r3(pre, NT), r3(l, NT), D[:, d, u % 2, :].rearrange("p (g t) -> p g t", g=NT)
                    whole, update, centre = (vecs[:, k, u, :] for k in range(3))
                    last, mid = p3[:, :, P - 1:P].rearrange("p g o -> p (g o)"), P // 2
                    if d == 0:
                        c = p3[:, :, mid - 1:mid].rearrange("p g o -> p (g o)")
                        nc.vector.tensor_tensor(D3, p3, bc(c, P), ALU.subtract)
                        nc.vector.tensor_copy(whole, last)
                        nc.vector.tensor_copy(centre, c)
                        nc.vector.tensor_tensor(update, last, c, ALU.subtract).then_inc(sem("vecs_raw"), 1)
                    else:
                        own.link(nc.vector.tensor_tensor(l, pre, l, ALU.subtract))
                        c = l3[:, :, mid:mid + 1].rearrange("p g o -> p (g o)")
                        nc.vector.tensor_tensor(D3, bc(c, P), l3, ALU.subtract)
                        nc.vector.tensor_copy(whole, last)
                        nc.vector.tensor_copy(update, c)
                        nc.vector.tensor_tensor(centre, last, c, ALU.subtract).then_inc(sem("vecs_raw"), 1)

                def ada(n):
                    to = mrow2[n % 2]
                    dve.wait_ge(sem(f"brow2_in{n % 2}"), 16 * (n // 2 + 1))
                    dve.wait_ge(sem("ada2_made"), n + 1)
                    if n >= 2:
                        dve.wait_ge(sem(f"mod2_out{n % 2}"), 16 * (n // 2))
                    add = nc.vector.tensor_tensor(to, bank(6 + n % 2)[0:2, :], brow2[n % 2], ALU.add)
                    if n in (4, 5):
                        own.link(add)
                        dve.wait_ge(sem("nrow2_in"), 32)
                        add = nc.vector.scalar_tensor_tensor(to, to, 1.0, nrow2[n % 2], ALU.add, ALU.mult)
                    add.then_inc(sem("mod2_ready"), 1)

                for u in range(4):
                    decay(u)
                    ada(2 * u)
                    ada(2 * u + 1)

            @block.tensor
            def _(pe):
                pe.wait_ge(sem("gate_w_in"), 32)

                def gates(u):
                    if u >= 2:
                        pe.wait_ge(sem("z_read"), u - 1)
                    for a in range(3):
                        last = nc.tensor.matmul(bank((u % 2) * 3 + a, 384), WG[:, u // 2, (u % 2) * P:(u % 2 + 1) * P],
                                                lrT[:, a * 384:(a + 1) * 384], start=True, stop=True)
                    last.then_inc(sem("z_made"), 1)

                def ada(n):
                    pe.wait_ge(sem(f"ada2_in{n % 3}"), 16 * (n // 3 + 1))
                    if n >= 2:
                        pe.wait_ge(sem("mod2_ready"), n - 1)
                    for j in range(KT):
                        last = nc.tensor.matmul(bank(6 + n % 2)[0:2, :], scT[:, j:2 * KT:KT], RING_B[n % 3][:, j, :],
                                                start=(j == 0), stop=(j == KT - 1))
                    last.then_inc(sem("ada2_made"), 1)

                gates(0)
                gates(1)
                for u in range(4):
                    ada(2 * u)
                    if u < 2:
                        gates(u + 2)
                    ada(2 * u + 1)

        with stage("pads_out seen_in") as block:
            kT_tile = lambda g: qkT[:, 2:4, ds(g * P, P)].unsqueeze(1).broadcast_to([P, 2, 2, P])
            qT_tile = lambda g: qkT[:, 0:2, ds(g * P, P)].unsqueeze(1).broadcast_to([P, 2, 2, P])
            D_tile = lambda g: D[:, :, :, ds(g * P, P)]
            r4 = lambda ap: ap.rearrange("p (d q t) -> p d q t", d=2, q=2)
            vec = lambda k, g: vecs[:, k, :, ds(g, 1)].rearrange("p u o -> p (u o)")

            @block.sync
            def _(sp):
                sp.wait_ge(sem("added"), 1)
                for d, name in enumerate(("new_sf", "new_sb")):
                    for half in range(2):
                        sp.dma_start(t_out[name][0, 0].rearrange("(q h) k v -> h k q v", h=2)[half],
                                     U[64 * half:64 * half + 64, 0, 2 * d:2 * d + 2, :]).then_inc(sem("out_states"), 16)
                sp.wait_ge(sem("out_states"), 64)

            @block.scalar
            def _(act):
                with act.Fori(0, NT) as g:
                    wait(act, sem("kf_made"), g)
                    nc.scalar.activation(r4(ek), D_tile(g), ACT.Exp, scale=-1.0 / 16).then_inc(sem("ek_made"), 1)
                    wait(act, sem("kf_transposed"), g + 1)
                    wait(act, sem("sums_made"), g)
                    nc.scalar.activation(kTM, bank(0), ACT.Copy).then_inc(sem("kTM_made"), 1)

            @block.gpsimd
            def _(pool):
                nc.gpsimd.memset(ar(27008, NT * 2 * H), 0.0).then_inc(sem("Sb_cleared"), 1)
                pool.wait_ge(sem("state_in"), 64)
                pool.wait_ge(sem("vecs_ready"), 1)
                pool.wait_ge(sem("Sb_cleared"), 1)
                with pool.Fori(0, NS) as i:
                    wait(pool, sem("stepped"), i)
                    for d, g in enumerate((i + 1, NS - i)):
                        for half in range(2):
                            rows = slice(64 * half, 64 * half + 64)
                            us = slice(2 * d, 2 * d + 2)
                            nc.gpsimd.tensor_tensor(Sb[rows, ds(g, 1), us, half, :].rearrange("p o u c -> p (o u) c"),
                                                    S[rows, us, :],
                                                    vecs[rows, 2, us, ds(g, 1)].broadcast_to([64, 2, P]),
                                                    ALU.mult).then_inc(sem("state_kept"), 1)

            @block.vector
            def _(dve):
                own = Chain(dve, sem("own_b2"))
                dve.wait_ge(sem("vecs_ready"), 1)
                with dve.Fori(0, NT) as g:
                    wait(dve, sem("ek_made"), g + 1)
                    wait(dve, sem("kf_transposed"), g)
                    nc.vector.tensor_tensor(r4(kf), kT_tile(g), r4(ek), ALU.mult).then_inc(sem("kf_made"), 1)
                    wait(dve, sem("sums_made"), g + 1)
                    for half in range(2):
                        rows = slice(64 * half, 64 * half + 64)
                        last = nc.vector.tensor_tensor(U[rows, ds(g, 1), :, :].rearrange("p o u c -> p (o u) c"),
                                                       PS[rows, H:3 * H].rearrange("p (u h c) -> p u h c", u=4, h=2)[:, :, half, :],
                                                       vecs[rows, 1, :, ds(g, 1)].broadcast_to([64, 4, P]), ALU.mult)
                    last.then_inc(sem("added"), 1)
                dve.wait_ge(sem("added"), NT)
                dve.wait_ge(sem("state_in"), 64)
                with dve.Fori(0, NS) as i:
                    own.start(i)
                    for d, g in enumerate((i + 1, NS - i)):
                        us = slice(2 * d, 2 * d + 2)
                        last = nc.vector.tensor_tensor(St[:, us, :], S[:, us, :], vecs[:, 0, us, ds(g, 1)].broadcast_to([P, 2, P]), ALU.mult)
                    own.link(last)
                    wait(dve, sem("state_kept"), i * 4 + 4)
                    for d, g in enumerate((i + 1, NS - i)):
                        us = slice(2 * d, 2 * d + 2)
                        last = nc.vector.tensor_tensor(S[:, us, :], St[:, us, :],
                                                       U[:, ds(g, 1), us, :].rearrange("p o u c -> p (o u) c"), ALU.add)
                    last.then_inc(sem("stepped"), 1)
                    wait(dve, sem("stepped"), i + 1)

            @block.tensor
            def _(pe):
                with pe.Fori(0, NT) as g:
                    wait(pe, sem("kf_made"), g + 1)
                    wait(pe, sem("kTM_made"), g)
                    for u in range(4):
                        last = nc.tensor.transpose(bank(0, P, u * P), kf[:, u * P:(u + 1) * P], ident)
                    last.then_inc(sem("kf_transposed"), 1)
                    wait(pe, sem("kTM_made"), g + 1)
                    wait(pe, sem("added"), g)
                    for u in range(4):
                        q = u % 2
                        last = nc.tensor.matmul(bank(1 + u // 2, 2 * P, q * 2 * P), kTM[:, u * P:(u + 1) * P],
                                                v_all[:, ds(g, 1), q * 2 * DV:(q + 1) * 2 * DV].rearrange("p o c -> p (o c)"),
                                                start=True, stop=True)
                    last.then_inc(sem("sums_made"), 1)

        with stage("pads_out") as block:
            @block.scalar
            def _(act):
                with act.Fori(0, NT) as g:
                    wait(act, sem("qk_decayed"), g)
                    nc.scalar.activation(r4(eq), D_tile(g), ACT.Exp, scale=1.0 / 16).then_inc(sem("eq_made"), 1)
                    nc.scalar.activation(r4(ekc), D_tile(g), ACT.Exp, scale=-1.0 / 16).then_inc(sem("ekc_made"), 1)
                    wait(act, sem("gla_made"), g + 1)
                    wait(act, sem("osq_read"), g)
                    nc.scalar.activation(osq.rearrange("p (a b) -> p a b", a=2),
                                         PS[:, 2 * H:4 * H].rearrange("p (a b) -> p a b", a=2)[:, :, 0:2 * P],
                                         ACT.Square).then_inc(sem("o_squared"), 1)

            @block.gpsimd
            def _(pool):
                for half in range(2):
                    nc.gpsimd.memset(sc[half], 0.0).then_inc(sem("sc_cleared"), 1)
                with pool.Fori(0, NT) as g:
                    wait(pool, sem("o_mean"), g + 1)
                    nc.gpsimd.tensor_tensor(ro4, vo4, negh[:, 0:4], ALU.pow).then_inc(sem("o_rstd"), 1)

            @block.vector
            def _(dve):
                own = Chain(dve, sem("own_c"))
                dve.wait_ge(sem("sc_cleared"), 2)
                dve.wait_ge(sem("seen_in"), 16)
                with dve.Fori(0, NT) as g:
                    own.start(g)
                    wait(dve, sem("ekc_made"), g + 1)
                    wait(dve, sem("gla_made"), g)
                    for d in range(2):
                        nc.vector.scalar_tensor_tensor(r4(qf)[:, d], qkT[:, 0:2, ds(g * P, P)], float(HD) ** -0.5, r4(eq)[:, d],
                                                       ALU.mult, ALU.mult)
                    nc.vector.tensor_tensor(r4(kfc), kT_tile(g), r4(ekc), ALU.mult).then_inc(sem("qk_decayed"), 1)
                    wait(dve, sem("gla_scored"), g + 1)
                    nc.vector.tensor_copy(spare[:, 0:1], ones[:, 0:1])
                    for half in range(2):
                        nc.vector.copy_predicated(sc[half], seen, bank(half)).then_inc(sem("gla_masked"), 1)
                    wait(dve, sem("o_squared"), g + 1)
                    nc.vector.tensor_reduce(so4, r3(osq, GH), AX.X, ALU.add).then_inc(sem("osq_read"), 1)
                    wait(dve, sem("osq_read"), g + 1)
                    nc.vector.tensor_scalar(vo4, so4, 1.0 / DV, EPS, ALU.mult, ALU.add).then_inc(sem("o_mean"), 1)
                    wait(dve, sem("o_rstd"), g + 1)
                    own.link(nc.vector.tensor_tensor(on.rearrange("p (a b c) -> p a b c", a=2, b=2),
                                                     PS[:, 2 * H:4 * H].rearrange("p (a b c) -> p a b c", a=2, b=4)[:, :, 0:2, :],
                                                     ro4.rearrange("p (a b) -> p a b", a=2).unsqueeze(3).broadcast_to([P, 2, 2, P]), ALU.mult))
                    gg = ga_all[:, ds(g, 1), :].rearrange("p o c -> p (o c)")
                    nc.vector.tensor_tensor(gg, on, gg, ALU.mult).then_inc(sem("gla_done"), 1)

            @block.tensor
            def _(pe):
                with pe.Fori(0, NT) as g:
                    wait(pe, sem("qk_decayed"), g + 1)
                    wait(pe, sem("gla_masked"), g * 2)
                    for half in range(2):
                        rows = slice(64 * half, 64 * half + 64)
                        for u in range(4):
                            last = nc.tensor.matmul(bank(half, P, u * P), kfc[rows, u * P:(u + 1) * P], qf[rows, u * P:(u + 1) * P],
                                                    start=True, stop=True)
                    last.then_inc(sem("gla_scored"), 1)
                    wait(pe, sem("gla_done"), g)
                    wait(pe, sem("gla_masked"), g * 2 + 2)
                    for q in range(2):
                        out = bank(2 + q, 2 * P)
                        for d in range(2):
                            u = 2 * d + q
                            nc.tensor.matmul(out, qf[:, u * P:(u + 1) * P],
                                             Sb[:, ds(g, 1), u, :, :].rearrange("p o h c -> p (o h c)"), start=(d == 0), stop=False)
                        for half in range(2):
                            h = 2 * q + half
                            for d in range(2):
                                u = 2 * d + q
                                last = nc.tensor.matmul(bank(2 + q, P, half * P), sc[half][:, u * P:(u + 1) * P],
                                                        v_all[:, ds(g, 1), h * DV:(h + 1) * DV].rearrange("p o c -> p (o c)"),
                                                        start=False, stop=(half == 1 and d == 1))
                    last.then_inc(sem("gla_made"), 1)

        SCALE = float(HD) ** -0.5
        RG = NH // NKV
        head = lambda hh: (hh // RG, hh % RG)
        with stage("pads_out mE_in w_out_in") as block:
            @block.sync
            def _(sp):
                for a in range(NC):
                    sp.dma_start(kc[:, a, :], t_in["cache_k"][0, 0, a * P:(a + 1) * P].rearrange("s h d -> s (h d)")).then_inc(sem("cache_in"), 16)
                    sp.dma_start(va[:, NT + a, :], t_in["cache_v"][0, 0, a * P:(a + 1) * P].rearrange("s h d -> s (h d)")).then_inc(sem("cache_in"), 16)
                for c in range(2):
                    for i, r in enumerate((2, 4, 3)):
                        sp.dma_start(mE[c][i], spread(mod_d[c, r])).then_inc(sem("mE_in"), 16)
                for j in range(KT):
                    sp.dma_start(w_out[:, j, :], w_out_v[:, j, :]).then_inc(sem("w_out_in"), 16)

            @block.gpsimd
            def _(pool):
                with pool.Fori(1, NT) as g:
                    wait(pool, sem("scored"), g * NH - NH)
                    nc.gpsimd.tensor_copy(r3(qst, 4), qaT[:, :, ds(g * P, P)]).then_inc(sem("q_staged"), 1)
                pool.wait_ge(sem("scored"), NS * NH)
                nc.gpsimd.memset(spare, 0.0).then_inc(sem("q_staged"), 1)

            @block.scalar
            def _(act):
                act.wait_ge(sem("kcT_made"), 1)
                nc.scalar.activation(kaT[:, TOK:TOK + NC * P], bank(7, NC * P), ACT.Copy).then_inc(sem("kcT_kept"), 1)
                act.wait_ge(sem("c_shifted"), 1)
                nc.scalar.activation(pr[0][:, 0:NH * P], pr[0][:, 0:NH * P], ACT.Exp, scale=SCALE).then_inc(sem("c_exp"), 1)
                act.wait_ge(sem("c_transposed"), 1)
                nc.scalar.activation(pT[0][:, 0:NH * P], PS[:, 2 * H:4 * H], ACT.Copy).then_inc(sem("c_pT"), 1)

                act.wait_ge(sem("max_made"), 1)
                nc.scalar.activation(pr[0], PS[:, 0:KEYS], ACT.Exp, bias=nmx[:, 0:1], scale=SCALE,
                                     accum_out=rs[:, 0:1]).then_inc(sem("exp_made"), 1)
                with act.Fori(0, NS) as t:
                    for hh in range(NH):
                        n = t * NH + hh
                        nx = (hh + 1) % NH
                        wait(act, sem("max_made"), n + 2)
                        wait(act, sem("p_transposed"), n * 3)
                        nc.scalar.activation(pr[nx % 2], PS[:, (nx % 2) * 3 * H:(nx % 2) * 3 * H + KEYS], ACT.Exp,
                                             bias=nmx[:, nx:nx + 1], scale=SCALE, accum_out=rs[:, nx:nx + 1]).then_inc(sem("exp_made"), 1)
                        wait(act, sem("p_transposed"), n * 3 + 2)
                        nc.scalar.activation(pT[hh % 2][:, H:2 * H], bank(6), ACT.Copy).then_inc(sem("pT_odd"), 1)

            @block.vector
            def _(dve):
                own = Chain(dve, sem("own_d"))
                dve.wait_ge(sem("c_scored"), 1)
                own.link(nc.vector.tensor_reduce(mx, r3(PS[:, 0:NH * P], NH), AX.X, ALU.max))
                nc.vector.tensor_tensor(r3(pr[0][:, 0:NH * P], NH), r3(PS[:, 0:NH * P], NH), bc(mx, P), ALU.subtract).then_inc(sem("c_shifted"), 1)
                dve.wait_ge(sem("c_exp"), 1)
                own.link(nc.vector.tensor_reduce(rs, r3(pr[0][:, 0:NH * P], NH), AX.X, ALU.add))
                own.link(nc.vector.reciprocal(rrs, rs))
                dve.wait_ge(sem("c_mixed"), 1)
                nc.vector.tensor_tensor(r3(oatt[:, 0, :], NH), r3(bank(4), NH), bc(rrs, HD), ALU.mult).then_inc(sem("c_done"), 1)

                own_l = Chain(dve, sem("own_dl"))

                def top(n, hh):
                    wait(dve, sem("scored"), n + 1)
                    own_l.link(nc.vector.tensor_reduce(mx[:, hh:hh + 1], PS[:, (hh % 2) * 3 * H:(hh % 2) * 3 * H + KEYS], AX.X, ALU.max))
                    nc.vector.tensor_scalar(nmx[:, hh:hh + 1], mx[:, hh:hh + 1], -SCALE, None, ALU.mult).then_inc(sem("max_made"), 1)

                top(0, 0)
                with dve.Fori(0, NS) as t:
                    own_l.start(t * 2 * NH + 1)

                    def finish(n, hh):
                        wait(dve, sem("mixed"), n + 1)
                        own_l.link(nc.vector.reciprocal(rrs[:, hh:hh + 1], rs[:, hh:hh + 1]))
                        nc.vector.tensor_scalar(oatt[:, ds(t + 1, 1), hh * HD:(hh + 1) * HD], bank(7, HD, hh * HD).unsqueeze(1),
                                                rrs[:, hh:hh + 1], None, ALU.mult).then_inc(sem("head_done"), 1)

                    for hh in range(NH):
                        n = t * NH + hh
                        wait(dve, sem("p_transposed"), n * 3 + 1)
                        nc.vector.tensor_copy(pT[hh % 2][:, 0:H], bank(6)).then_inc(sem("pT_even"), 1)
                        top(n + 1, (hh + 1) % NH)
                        if hh >= 1:
                            finish(n - 1, hh - 1)
                        wait(dve, sem("p_transposed"), n * 3 + 3)
                        nc.vector.tensor_copy(pT[hh % 2][:, 2 * H:KEYS], bank(6, 2 * P)).then_inc(sem("pT_even"), 1)
                    finish(n, NH - 1)

            @block.tensor
            def _(pe):
                pe.wait_ge(sem("cache_in"), 16 * 2 * NC)
                for a in range(NC):
                    last = nc.tensor.transpose(bank(7, P, a * P), kc[:, a, :], ident)
                last.then_inc(sem("kcT_made"), 1)
                for hh in range(NH):
                    v, r = head(hh)
                    rows = slice(HD * v, HD * v + HD)
                    last = nc.tensor.matmul(PS[:, hh * P:(hh + 1) * P], qaT[rows, r, 0:P], kaT[rows, 0:P], start=True, stop=True)
                last.then_inc(sem("c_scored"), 1)
                pe.wait_ge(sem("c_exp"), 1)
                for hh in range(NH):
                    last = nc.tensor.transpose(PS[:, 2 * H + hh * P:2 * H + (hh + 1) * P], pr[0][:, hh * P:(hh + 1) * P], ident)
                last.then_inc(sem("c_transposed"), 1)
                pe.wait_ge(sem("c_pT"), 1)
                for hh in range(NH):
                    v, r = head(hh)
                    last = nc.tensor.matmul(bank(4, HD, hh * HD), pT[0][:, hh * P:(hh + 1) * P], va[:, 0, v * HD:(v + 1) * HD], start=True, stop=True)
                last.then_inc(sem("c_mixed"), 1)
                pe.wait_ge(sem("c_done"), 1)
                pe.wait_ge(sem("kcT_kept"), 1)

                def score(n, hh, tile_count):
                    v, r = head(hh)
                    rows = slice(HD * v, HD * v + HD)
                    if hh == 0:
                        wait(pe, sem("q_staged"), tile_count)
                    for a, w in ((0, H), (1, H), (2, KEYS - 2 * H)):
                        last = nc.tensor.matmul(bank((hh % 2) * 3 + a, w), qst[rows, r * P:(r + 1) * P],
                                                kaT[rows, P + a * H:P + a * H + w], start=True, stop=True)
                    last.then_inc(sem("scored"), 1)

                score(0, 0, 1)
                with pe.Fori(0, NS) as t:
                    for hh in range(NH):
                        n = t * NH + hh

                        def turn(a, k0, k1):
                            for k in range(k0, k1):
                                last = nc.tensor.transpose(bank(6, P, (k - k0) * P), pr[hh % 2][:, k * P:(k + 1) * P], ident)
                            last.then_inc(sem("p_transposed"), 1)

                        def mix(n_, h_, k0, k1):
                            v, r = head(h_)
                            for k in range(k0, k1):
                                last = nc.tensor.matmul(bank(7, HD, h_ * HD), pT[h_ % 2][:, k * P:(k + 1) * P],
                                                        va[:, 1 + k, v * HD:(v + 1) * HD], start=(k == 0), stop=(k == NS + NC - 1))
                            return last

                        wait(pe, sem("exp_made"), n)
                        score(n + 1, (hh + 1) % NH, t + 2)
                        wait(pe, sem("exp_made"), n + 1)
                        wait(pe, sem("pT_even"), n * 2)
                        turn(0, 0, 4)
                        if hh >= 1:
                            mix(n - 1, hh - 1, 0, 6)
                        wait(pe, sem("pT_even"), n * 2 + 1)
                        turn(1, 4, 8)
                        if hh >= 1:
                            mix(n - 1, hh - 1, 6, NS + NC).then_inc(sem("mixed"), 1)
                        wait(pe, sem("pT_odd"), n + 1)
                        turn(2, 8, NS + NC)
                    wait(pe, sem("pT_even"), n * 2 + 2)
                    mix(n, NH - 1, 0, NS + NC).then_inc(sem("mixed"), 1)

        w_gu_v = t_in["w_gu"][0].rearrange("e (j p) n -> e p j n", p=P)
        w_dn_v = t_in["w_down"][0].rearrange("e (j p) n -> e p j n", p=P)

        def chunk_src(e, c):
            if c < 4:
                lo = (c % 2) * FF + (c // 2) * H
                return w_gu_v[ds(e, 1), :, :, lo:lo + H].rearrange("o p j n -> (o p) j n")
            j0 = (c - 4) * KT // 2
            return w_dn_v[ds(e, 1), :, j0:j0 + KT // 2, :].rearrange("o p j n -> (o p) j n")

        def chunk_dst(c):
            return r3(wc[c], KT) if c < 4 else r3(wc[c], KT // 2)

        EARLY = 3
        with stage("w_in0 w_in1 w_in2") as block:
            def steps(front, back, eng):
                front(0, False)
                with eng.Fori(1, NT) as g:
                    front(g, True)
                    back(g - 1)

            @block.sync
            def _(sp):
                sp.dma_start(w_rt, w_rt_v).then_inc(sem("w_rt_in"), 16)

                def tile(g, x_src):
                    wait(sp, sem("x1_made"), g)
                    sp.dma_start(xr, x_src).then_inc(sem("xr_in"), 16)
                    wait(sp, sem("x1_made"), g + 1)
                    sp.dma_start(x1_d[ds(g * P, P), :], x1).then_inc(sem("x1_out"), 16)
                    wait(sp, sem("h2_made"), g + 1)
                    sp.dma_start(h2_d[ds(g * P, P), :], h2).then_inc(sem("h2_out"), 16)

                tile(0, x_ctx)
                with sp.Fori(1, NT) as g:
                    tile(g, x_lat[ds(g * P - P, P), :])
                sp.wait_ge(sem("x1_out"), 16 * NT)
                sp.wait_ge(sem("h2_out"), 16 * NT)
                sp.wait_ge(sem("zeros_out"), 16 * (NT + 2))

            @block.scalar
            def _(act):
                for c in range(EARLY):
                    act.dma_start(chunk_dst(c), chunk_src(0, c)).then_inc(sem(f"w_in{c}"), 16)
                act.wait_ge(sem("zeroed"), 1)
                for a in range(NT + 1):
                    act.dma_start(moe_d[a * P:(a + 1) * P, :], zeros).then_inc(sem("zeros_out"), 16)
                act.dma_start(h2_d[TOK:TOK + PADS, :], zeros).then_inc(sem("zeros_out"), 16)

                def front(g, latent):
                    wait(act, sem("mix_transposed"), g + 1)
                    wait(act, sem("projected"), g)
                    nc.scalar.activation(mixT, PS[:, 2 * H:4 * H], ACT.Copy).then_inc(sem("mixT_made"), 1)
                    if not latent:
                        square(g)

                def square(g):
                    wait(act, sem("x1_made"), g + 1)
                    nc.scalar.activation(junkE, x1, ACT.Square, accum_out=ss).then_inc(sem("x1_squared"), 1)

                def back(b, last=False):
                    wait(act, sem("h2_transposed"), b + 1)
                    wait(act, sem("routed"), b)
                    nc.scalar.activation(h2T, PS[:, 4 * H:6 * H], ACT.Copy).then_inc(sem("h2T_made"), 1)
                    if not last:
                        square(b + 1)
                    wait(act, sem("top_made"), b + 1)
                    nc.scalar.activation(exg, top8[:, 0:TOPK], ACT.Exp, bias=ntop, accum_out=gsum).then_inc(sem("gates_exp"), 1)

                steps(front, back, act)
                back(NT - 1, last=True)

            @block.gpsimd
            def _(pool):
                nc.gpsimd.memset(zeros, 0.0).then_inc(sem("zeroed"), 1)
                pool.wait_ge(sem("pads_out"), 16)

                def stage_mix(g):
                    wait(pool, sem("mix_transposed"), g)
                    nc.gpsimd.tensor_copy(mixs[:, 0:H], ga_all[:, ds(g, 1), :].rearrange("p o c -> p (o c)"))
                    nc.gpsimd.tensor_copy(mixs[:, H:2 * H], oatt[:, ds(g, 1), :].rearrange("p o c -> p (o c)")).then_inc(sem("mix_staged"), 1)

                def norm(g):
                    wait(pool, sem("x1_mean"), g + 1)
                    nc.gpsimd.tensor_tensor(rstd, msq, negh[:, 0:1], ALU.pow).then_inc(sem("x1_rstd"), 1)

                def scatter(b):
                    wait(pool, sem("entries_made"), b + 1)
                    settle(pool, "pool_steps")
                    for k in range(TOPK):
                        pool.indirect_dma_start(out=list_d, out_offset=bass.IndirectOffsetOnAxis(ap=sloti[:, k:k + 1].bitcast(U32), axis=0),
                                                in_=ent[:, 2 * k:2 * k + 2], in_offset=None).then_inc(sem("listed_out"), 16)

                stage_mix(0)
                stage_mix(1)
                norm(0)
                with pool.Fori(1, NT - 1) as g:
                    stage_mix(g + 1)
                    scatter(g - 1)
                    norm(g)
                scatter(NT - 2)
                norm(NT - 1)
                scatter(NT - 1)
                pool.wait_ge(sem("listed_out"), 16 * TOPK * NT)

            @block.vector
            def _(dve):
                own = Chain(dve, sem("own_e"))
                FRONT_LINKS, BACK_LINKS = 2, 12
                def front(g, latent):
                    gate = mE[0 if latent else 1][0]
                    wait(dve, sem("projected"), g + 1)
                    wait(dve, sem("x1_out"), g * 16)
                    own.link(nc.vector.tensor_tensor(x1, PS[:, 0:DM], gate, ALU.mult))
                    wait(dve, sem("xr_in"), g * 16 + 16)
                    nc.vector.tensor_tensor(x1, x1, xr, ALU.add).then_inc(sem("x1_made"), 1)

                def norm(g, latent):
                    _, scale, shift = mE[0 if latent else 1]
                    wait(dve, sem("x1_squared"), g + 1)
                    nc.vector.tensor_scalar(msq, ss, 1.0 / DM, EPS, ALU.mult, ALU.add).then_inc(sem("x1_mean"), 1)
                    wait(dve, sem("x1_rstd"), g + 1)
                    wait(dve, sem("h2_out"), g * 16)
                    wait(dve, sem("h2_transposed"), g)
                    own.link(nc.vector.scalar_tensor_tensor(h2, x1, rstd, scale, ALU.mult, ALU.mult))
                    nc.vector.tensor_tensor(h2, h2, shift, ALU.add).then_inc(sem("h2_made"), 1)

                def back(b):
                    wait(dve, sem("routed"), b + 1)
                    own.link(nc.vector.tensor_tensor(logit, bank(6, NE), brt, ALU.add))
                    settle(dve, "dve_steps")
                    own.link(nc.vector.max(out=top8, in_=logit))
                    settle(dve, "dve_steps")
                    own.link(nc.vector.max_index(out=top8i, in_max=top8, in_values=logit))
                    nc.vector.tensor_scalar(ntop, top8[:, 0:1], -1.0, None, ALU.mult).then_inc(sem("top_made"), 1)
                    own.link(nc.vector.tensor_copy(idxf, top8i))
                    own.link(nc.vector.tensor_scalar(picked, expert, idxf[:, 0:1], None, ALU.is_equal))
                    for k in range(1, TOPK):
                        ins = nc.vector.scalar_tensor_tensor(picked, expert, idxf[:, k:k + 1], picked, ALU.is_equal, ALU.add)
                        if k < TOPK - 1:
                            own.link(ins)
                    ins.then_inc(sem("picked_made"), 1)
                    wait(dve, sem("gates_exp"), b + 1)
                    own.link(nc.vector.reciprocal(gcp, gsum))
                    wait(dve, sem("listed_out"), b * 64)
                    own.link(nc.vector.tensor_scalar(gates, exg, gcp, None, ALU.mult))
                    own.link(nc.vector.tensor_copy(ent.bitcast(F32)[:, 1:8:2], gates))
                    nc.vector.tensor_copy(ent[:, 0:8:2], tokid[:, ds(b, 1)].broadcast_to([P, TOPK]))
                    wait(dve, sem("placed"), b + 1)
                    own.link(nc.vector.scalar_tensor_tensor(place, expert, float(LISTW), bank(7, NE), ALU.mult, ALU.add))
                    nc.vector.tensor_tensor(pickedsum, pickedsum, picked, ALU.add)
                    for k in range(TOPK):
                        ins = nc.vector.scalar_tensor_tensor(spares[:, k], expert, idxf[:, k:k + 1], place, ALU.is_equal, ALU.mult,
                                                             accum_out=slotf[:, k:k + 1])
                    own.link(ins)
                    nc.vector.tensor_copy(sloti, slotf).then_inc(sem("entries_made"), 1)

                front(0, False)
                norm(0, False)
                assert own.n == FRONT_LINKS
                with dve.Fori(1, NT) as g:
                    own.start(FRONT_LINKS + (g - 1) * (FRONT_LINKS + BACK_LINKS))
                    front(g, True)
                    back(g - 1)
                    norm(g, True)
                    assert own.n == FRONT_LINKS + BACK_LINKS, own.n
                own.start(FRONT_LINKS + (NT - 1) * (FRONT_LINKS + BACK_LINKS))
                back(NT - 1)
                dve.wait_ge(sem("counted"), 1)
                own.link(nc.vector.tensor_scalar(cnti, bank(6, NE), float(P - 1), None, ALU.add))
                own.link(nc.vector.tensor_scalar(cnti, cnti, 7, None, ALU.arith_shift_right))
                own.link(nc.vector.tensor_scalar(ntl, cnti, 1.0, None, ALU.max))
                own.link(nc.vector.memset(tstart[:, 0:1], 0))
                own.link(nc.vector.tensor_tensor_scan(tstartf, ones[:, 0:NE], ntl, 0.0, ALU.mult, ALU.add))
                nc.vector.tensor_copy(tstart[:, 1:NE + 1], tstartf).then_inc(sem("tiles_known"), 1)

            @block.tensor
            def _(pe):
                pe.wait_ge(sem("mE_in"), 16 * 6)
                pe.wait_ge(sem("w_out_in"), 16 * KT)
                pe.wait_ge(sem("w_rt_in"), 16)

                def front(g, latent):
                    wait(pe, sem("mix_staged"), g + 1)
                    wait(pe, sem("mixT_made"), g)
                    for j in range(KT):
                        last = nc.tensor.transpose(PS[:, 2 * H + j * P:2 * H + (j + 1) * P], mixs[:, j * P:(j + 1) * P], ident)
                    last.then_inc(sem("mix_transposed"), 1)
                    wait(pe, sem("mixT_made"), g + 1)
                    wait(pe, sem("x1_made"), g)
                    for a in range(2):
                        for j in range(KT):
                            last = nc.tensor.matmul(bank(a), mixT[:, j * P:(j + 1) * P], w_out[:, j, a * H:(a + 1) * H],
                                                    start=(j == 0), stop=(j == KT - 1))
                    last.then_inc(sem("projected"), 1)

                def back(b):
                    wait(pe, sem("h2_made"), b + 1)
                    wait(pe, sem("h2T_made"), b)
                    for j in range(KT):
                        last = nc.tensor.transpose(PS[:, 4 * H + j * P:4 * H + (j + 1) * P], h2[:, j * P:(j + 1) * P], ident)
                    last.then_inc(sem("h2_transposed"), 1)
                    wait(pe, sem("h2T_made"), b + 1)
                    wait(pe, sem("top_made"), b)
                    for j in range(KT):
                        last = nc.tensor.matmul(bank(6, NE), h2T[:, j * P:(j + 1) * P], w_rt[:, j, :], start=(j == 0), stop=(j == KT - 1))
                    last.then_inc(sem("routed"), 1)
                    wait(pe, sem("picked_made"), b + 1)
                    wait(pe, sem("entries_made"), b)
                    nc.tensor.matmul(bank(7, NE), upper, picked, start=True, stop=False)
                    nc.tensor.matmul(bank(7, NE), ones, pickedsum, start=False, stop=True).then_inc(sem("placed"), 1)

                steps(front, back, pe)
                back(NT - 1)
                pe.wait_ge(sem("entries_made"), NT)
                nc.tensor.matmul(bank(6, NE), ones, pickedsum, start=True, stop=True).then_inc(sem("counted"), 1)

        def expert_tiles(eng, body, each=None):
            with eng.Fori(0, NE) as e:
                s = eng.value_load(tstart[0:1, ds(e, 1)], min_val=0, max_val=TOK * TOPK // P + NE)
                n = eng.value_load(tstart[0:1, ds(e + 1, 1)], min_val=0, max_val=TOK * TOPK // P + NE)
                if each:
                    each(e, s)
                with eng.Fori(s, n) as j:
                    body(e, j, s)

        with stage("") as block:
            @block.sync
            def _(sp):
                def load(e, c):
                    sp.dma_start(chunk_dst(c), chunk_src(e, c)).then_inc(sem(f"w_in{c}"), 16)

                def biases(e, which):
                    if which == 0:
                        sp.dma_start(bias[:, 0:2 * FF], t_in["b_gu"][0, ds(e, 1), :].rearrange("o n -> (o n)").partition_broadcast(P)).then_inc(sem("b_gu_in"), 16)
                    else:
                        sp.dma_start(bias[:, 2 * FF:2 * FF + DM], t_in["b_down"][0, ds(e, 1), :].rearrange("o n -> (o n)").partition_broadcast(P)).then_inc(sem("b_dn_in"), 16)

                load(0, 3)
                biases(0, 0)
                load(0, 4)
                load(0, 5)
                biases(0, 1)
                with sp.Fori(1, NE) as e:
                    s = sp.value_load(tstart[0:1, ds(e, 1)], min_val=0, max_val=TOK * TOPK // P + NE)
                    for c in range(CHUNKS):
                        wait(sp, sem(f"used{c}"), s)
                        load(e, c)
                        if c == 3:
                            wait(sp, sem("gu_biased"), s * 2)
                            biases(e, 0)
                    wait(sp, sem("y_biased"), s)
                    biases(e, 1)

            @block.gpsimd
            def _(pool):
                nc.gpsimd.memset(yo, 0.0).then_inc(sem("y_made"), 1)
                nc.gpsimd.tensor_scalar(current.bitcast(I32)[:, 0:1], tokid[:, NT - 1:NT], float(P), None, ALU.add).then_inc(sem("first_set"), 1)
                pool.wait_ge(sem("first_set"), 1)

                def add_up(j):
                    wait(pool, sem("y_made"), j + 1)
                    settle(pool, "pool_steps")
                    pool.indirect_dma_start(out=moe_d, out_offset=bass.IndirectOffsetOnAxis(ap=current.bitcast(U32)[:, 0:1], axis=0),
                                            in_=yo, in_offset=None, compute_op=ALU.add).then_inc(sem("added_up"), 16)

                def gather(j):
                    wait(pool, sem("x_turned"), j * 2)
                    settle(pool, "pool_steps")
                    pool.indirect_dma_start(out=xg, out_offset=None, in_=h2_d,
                                            in_offset=bass.IndirectOffsetOnAxis(ap=listed.bitcast(U32)[:, 0:1], axis=0)).then_inc(sem("gathered"), 16)

                def body(e, j, s):
                    wait(pool, sem("taken"), j)
                    row = nc.s_assert_within(e * LISTW + (j - s) * P, 0, (NE - 1) * LISTW + TOK - P,
                                             skip_runtime_bounds_check_because="an expert has at most TOK rows, in TOK / 128 tiles")
                    pool.dma_start(listed, list_d[ds(row, P), :]).then_inc(sem("listed_in"), 16)
                    wait(pool, sem("listed_in"), j * 16 + 16)
                    gather(j)
                    add_up(j)
                    wait(pool, sem("added_up"), j * 16 + 16)
                    settle(pool, "pool_steps")
                    nc.gpsimd.tensor_copy(current, listed.bitcast(F32)).then_inc(sem("taken"), 1)

                expert_tiles(pool, body)
                T = pool.value_load(tstart[0:1, NE:NE + 1], min_val=0, max_val=TOK * TOPK // P + NE)
                gather(T)
                add_up(T)
                wait(pool, sem("added_up"), T * 16 + 16)
                wait(pool, sem("gathered"), T * 16 + 16)

            @block.scalar
            def _(act):
                def turned_x(j, half):
                    wait(act, sem("x_turned"), j * 2 + half + 1)
                    nc.scalar.activation(xT[:, half * H:(half + 1) * H], bank(7), ACT.Copy).then_inc(sem("xT_made"), 1)

                def turned_act(j, half):
                    wait(act, sem("act_turned"), j * 2 + half + 1)
                    nc.scalar.activation(actT[:, half * H:(half + 1) * H], bank(6), ACT.Copy).then_inc(sem("actT_made"), 1)

                def sigmoid(j, half):
                    wait(act, sem("g_made"), j * 2 + half + 1)
                    wait(act, sem("act_made"), j * 2 + half)
                    nc.scalar.activation(sgm, gw[:, half * H:(half + 1) * H], ACT.Sigmoid, scale=1.702).then_inc(sem("sig_made"), 1)

                turned_x(0, 0)
                turned_x(0, 1)

                def body(e, j, s):
                    sigmoid(j, 0)
                    turned_act(j, 0)
                    turned_x(j + 1, 0)
                    sigmoid(j, 1)
                    turned_act(j, 1)
                    turned_x(j + 1, 1)
                    wait(act, sem("y_biased"), j + 1)
                    wait(act, sem("taken"), j + 1)
                    nc.scalar.activation(yo, yo, ACT.Copy, scale=current[:, 1:2]).then_inc(sem("y_made"), 1)

                expert_tiles(act, body)

            @block.vector
            def _(dve):
                own = Chain(dve, sem("own_f"))
                LINKS = 6

                def body(e, j, s):
                    own.start(j * LINKS)
                    for half in range(2):
                        cols = slice(half * H, (half + 1) * H)
                        g_, u_ = gw[:, cols], uw[:, cols]
                        if half == 0:
                            wait(dve, sem("b_gu_in"), e * 16 + 16)
                        wait(dve, sem(f"used{2 * half}"), j + 1)
                        own.link(nc.vector.tensor_tensor(g_, bank(2 * half), bias[:, cols], ALU.add))
                        nc.vector.tensor_scalar(g_, g_, 7.0, None, ALU.min).then_inc(sem("g_made"), 1)
                        wait(dve, sem(f"used{2 * half + 1}"), j + 1)
                        nc.vector.tensor_tensor(u_, bank(2 * half + 1), bias[:, FF + half * H:FF + (half + 1) * H], ALU.add).then_inc(sem("gu_biased"), 1)
                        wait(dve, sem("gu_biased"), j * 2 + half + 1)
                        own.link(nc.vector.tensor_scalar(u_, u_, 7.0, -7.0, ALU.min, ALU.max))
                        own.link(nc.vector.scalar_tensor_tensor(u_, u_, 1.0, g_, ALU.add, ALU.mult))
                        wait(dve, sem("sig_made"), j * 2 + half + 1)
                        nc.vector.tensor_tensor(act[:, cols], u_, sgm, ALU.mult).then_inc(sem("act_made"), 1)
                    wait(dve, sem("b_dn_in"), e * 16 + 16)
                    wait(dve, sem("used5"), j + 1)
                    wait(dve, sem("added_up"), j * 16 + 16)
                    nc.vector.tensor_tensor(yo, PS[:, 4 * H:6 * H], bias[:, 2 * FF:2 * FF + DM], ALU.add).then_inc(sem("y_biased"), 1)

                expert_tiles(dve, body)

            @block.tensor
            def _(pe):
                def turn_x(j, half):
                    if half == 0:
                        wait(pe, sem("gathered"), j * 16 + 16)
                    wait(pe, sem("xT_made"), j * 2 + half)
                    for k in range(4):
                        c = half * 4 + k
                        last = nc.tensor.transpose(bank(7, P, k * P), xg[:, c * P:(c + 1) * P], ident)
                    last.then_inc(sem("x_turned"), 1)

                def turn_act(j, half):
                    wait(pe, sem("act_made"), j * 2 + half + 1)
                    wait(pe, sem("actT_made"), j * 2 + half)
                    for k in range(4):
                        c = half * 4 + k
                        last = nc.tensor.transpose(bank(6, P, k * P), act[:, c * P:(c + 1) * P], ident)
                    last.then_inc(sem("act_turned"), 1)

                turn_x(0, 0)
                turn_x(0, 1)

                def body(e, j, s):
                    wait(pe, sem("xT_made"), j * 2 + 2)
                    for c in range(4):
                        wait(pe, sem(f"w_in{c}"), e * 16 + 16)
                        if c in (0, 2):
                            wait(pe, sem("gu_biased"), j * 2)
                        for k in range(KT):
                            last = nc.tensor.matmul(bank(c), xT[:, k * P:(k + 1) * P], chunk_dst(c)[:, k, :], start=(k == 0), stop=(k == KT - 1))
                        last.then_inc(sem(f"used{c}"), 1)
                    turn_act(j, 0)
                    turn_x(j + 1, 0)
                    wait(pe, sem("y_biased"), j)
                    for half in range(2):
                        wait(pe, sem(f"w_in{4 + half}"), e * 16 + 16)
                        wait(pe, sem("actT_made"), j * 2 + half + 1)
                        for a in range(2):
                            for k in range(4):
                                last = nc.tensor.matmul(bank(4 + a), actT[:, (half * 4 + k) * P:(half * 4 + k + 1) * P],
                                                        chunk_dst(4 + half)[:, k, a * H:(a + 1) * H],
                                                        start=(half == 0 and k == 0), stop=(half == 1 and k == 3))
                        last.then_inc(sem(f"used{4 + half}"), 1)
                        if half == 0:
                            turn_act(j, 1)
                            turn_x(j + 1, 1)

                expert_tiles(pe, body)

        with stage("") as block:
            @block.sync
            def _(sp):
                for c in range(2):
                    sp.dma_start(mG[c], spread(mod_d[c, 5])).then_inc(sem("mG_in"), 16)
                sp.dma_start(fn, spread(t_in["final_norm"])).then_inc(sem("mG_in"), 16)

                def load(g, slot):
                    wait(sp, sem("final_made"), g - 1)
                    sp.dma_start(ys[slot], moe_d[ds(g * P, P), :]).then_inc(sem(f"ys_in{slot}"), 16)
                    sp.dma_start(xf[slot], x1_d[ds(g * P, P), :]).then_inc(sem(f"ys_in{slot}"), 16)

                for g in range(2):
                    sp.dma_start(ys[g], moe_d[g * P:(g + 1) * P, :]).then_inc(sem(f"ys_in{g}"), 16)
                    sp.dma_start(xf[g], x1_d[g * P:(g + 1) * P, :]).then_inc(sem(f"ys_in{g}"), 16)
                with sp.Fori(0, NS // 2 - 1) as i:
                    load(i * 2 + 2, 0)
                    load(i * 2 + 3, 1)
                load(NT - 1, 0)

            @block.scalar
            def _(act):
                def body(g, slot, n):
                    wait(act, sem("final_summed"), g + 1)
                    nc.scalar.activation(ys[slot], xf[slot], ACT.Square, accum_out=ss).then_inc(sem("final_squared"), 1)
                    wait(act, sem("final_made"), g + 1)
                    to = t_out["y_prompt"][0] if n is None else t_out["y_sample"][0, ds(g * P - P, P), :]
                    act.dma_start(to, yf[slot]).then_inc(sem(f"y_out{slot}"), 16)

                body(0, 0, None)
                with act.Fori(0, NS // 2) as i:
                    body(i * 2 + 1, 1, 0)
                    body(i * 2 + 2, 0, 0)
                act.wait_ge(sem("y_out0"), 16 * (NS // 2 + 1))
                act.wait_ge(sem("y_out1"), 16 * (NS // 2))

            @block.gpsimd
            def _(pool):
                with pool.Fori(0, NT) as g:
                    wait(pool, sem("final_mean"), g + 1)
                    nc.gpsimd.tensor_tensor(rstd, msq, negh[:, 0:1], ALU.pow).then_inc(sem("final_rstd"), 1)

            @block.vector
            def _(dve):
                own = Chain(dve, sem("own_g"))
                dve.wait_ge(sem("mG_in"), 48)

                def body(g, slot, n, cond):
                    own.start(g)
                    wait(dve, sem(f"ys_in{slot}"), n * 32)
                    own.link(nc.vector.tensor_tensor(ys[slot], ys[slot], mG[cond], ALU.mult))
                    nc.vector.tensor_tensor(xf[slot], xf[slot], ys[slot], ALU.add).then_inc(sem("final_summed"), 1)
                    wait(dve, sem("final_squared"), g + 1)
                    nc.vector.tensor_scalar(msq, ss, 1.0 / DM, EPS, ALU.mult, ALU.add).then_inc(sem("final_mean"), 1)
                    wait(dve, sem("final_rstd"), g + 1)
                    wait(dve, sem(f"y_out{slot}"), n * 16 - 16)
                    nc.vector.scalar_tensor_tensor(yf[slot], xf[slot], rstd, fn, ALU.mult, ALU.mult).then_inc(sem("final_made"), 1)

                body(0, 0, 1, 1)
                with dve.Fori(0, NS // 2) as i:
                    body(i * 2 + 1, 1, i + 1, 0)
                    body(i * 2 + 2, 0, i + 2, 0)


def constants(NS, NT, NE, LISTW, HD, grid_w=64, theta=10000.0):
    import numpy as np

    out = {"ident": np.eye(P, dtype=np.float32)}
    col, row = np.arange(P)[None, :], np.arange(P)[:, None]
    out["upper"] = (col > row).astype(np.float32)
    see = np.stack([np.stack([row <= col] * 2, 1), np.stack([row >= col] * 2, 1)], 1)
    out["seen"] = see.astype(np.int32).reshape(P, 4 * P)
    out["keep"] = (np.arange(NT * P) % P != 0).astype(np.float32)
    out["tokid"] = (row + P * np.arange(NT)[None, :]).astype(np.float32)
    out["expert_id"] = np.arange(NE, dtype=np.float32)
    pads = np.zeros((NE * LISTW, 2), np.int32)
    pads[:, 0] = NT * P + np.arange(NE * LISTW) % P
    out["list_pads"] = pads
    t = np.arange(NS * P)
    inv = (1.0 / (theta ** (np.arange(HD // 4, dtype=np.float32) / np.float32(HD // 4)))).astype(np.float32)
    ang = np.concatenate([(t // grid_w)[:, None].astype(np.float32) * inv, (t % grid_w)[:, None].astype(np.float32) * inv], 1)
    cos, sin = np.cos(ang).astype(np.float32), np.sin(ang).astype(np.float32)
    out["rope"] = np.concatenate([np.repeat(cos, 2, 1), np.stack([-sin, sin], 2).reshape(NS * P, HD)], 1).astype(np.float32)
    return {k: np.ascontiguousarray(v) for k, v in out.items()}


_INS = ["x_prompt", "x_sample", "c", "cache_k", "cache_v", "state_gla_fwd", "state_gla_bwd", "c_ctx", "w_ada", "b_ada",
        "norm_mix", "w_in", "w_gate_f", "b_gate_f", "w_gate_b", "b_gate_b", "gla_norm", "q_norm", "k_norm", "w_out",
        "norm_ffn", "w_router", "b_router", "w_gu", "b_gu", "w_down", "b_down", "final_norm"]
_OUTS = [("y_prompt", (1, 128, 1024)), ("y_sample", (1, 1024, 1024)), ("new_k", (1, 1, 128, 2, 64)),
         ("new_v", (1, 1, 128, 2, 64)), ("new_sf", (1, 1, 4, 64, 128)), ("new_sb", (1, 1, 4, 64, 128))]


def kernel(**inputs):
    import numpy as np
    import concourse.bacc as bacc
    from concourse.bass_utils import run_bass_kernel_spmd

    nc = bacc.Bacc("TRN2", target_bir_lowering=False, num_devices=1)
    arrays = {n: np.ascontiguousarray(inputs[n]) for n in _INS}
    arrays.update(constants(8, 9, 32, 1152, 64))
    t_in, t_out, given = {}, {}, {}
    for n, a in arrays.items():
        given[f"in_{n}"] = a
        t_in[n] = nc.dram_tensor(f"in_{n}", a.shape, mybir.dt.from_np(a.dtype), kind="ExternalInput").ap()
    for n, shape in _OUTS:
        t_out[n] = nc.dram_tensor(f"out_{n}", shape, mybir.dt.float32, kind="ExternalOutput").ap()
    trunk_kernel(nc, t_in, t_out)
    r = run_bass_kernel_spmd(nc, [given], core_ids=[0])
    return tuple(r.results[0][f"out_{n}"] for n, _ in _OUTS)
```

```python
import concourse.bass as bass
from concourse import mybir
from contextlib import ExitStack, contextmanager

P = 128


class Chain:

    def __init__(self, eng, sem):
        self.eng, self.sem, self.base, self.n = eng, sem, 0, 0

    def start(self, base=0):
        self.base, self.n = base, 0

    def link(self, ins):
        ins.then_inc(self.sem, 1)
        self.n += 1
        self.eng.wait_ge(self.sem, self.base + self.n)


def trunk_kernel(nc, t_in, t_out):
    F32, I32, U32 = mybir.dt.float32, mybir.dt.int32, mybir.dt.uint32
    ALU, ACT, AX = mybir.AluOpType, mybir.ActivationFunctionType, mybir.AxisListType
    ds = bass.ds

    DM = t_in["x_sample"].shape[2]
    KT = DM // P
    NS = t_in["x_sample"].shape[1] // P
    NT = NS + 1
    TOK = NT * P
    DIN = t_in["w_in"].shape[2]
    HD = t_in["q_norm"].shape[1]
    NH, GH, DV = 8, 4, P
    NKV = t_in["cache_k"].shape[3]
    NC = t_in["cache_k"].shape[2] // P
    RANK = t_in["w_gate_f"].shape[1]
    NE = t_in["w_router"].shape[2]
    TOPK = 4
    FF = t_in["w_down"].shape[2]
    EPS = 1e-6
    H = 512
    KEYS = (NS + NC) * P
    C_LR, C_QB, C_KB = 1536, 1568, 2080
    LISTW = TOK
    PADS = P
    CHUNKS = 6
    RAW_SLOTS = 4
    HI_AHEAD, LO_AHEAD = 4, 3
    MAX_TILES = TOK * TOPK // P + NE

    hid = lambda name, shape, dt=F32: nc.dram_tensor(name, shape, dt, kind="Internal").ap()
    mod_d = hid("mod_rows", (2, 6, DM))
    x1_d = hid("x_after_mixing", (TOK, DM))
    h2_d = hid("expert_inputs", (TOK + PADS, DM))
    moe_d = hid("expert_sums", (TOK + PADS, DM))
    list_d = hid("expert_lists", (NE * LISTW, 2), I32)

    x_lat = t_in["x_sample"][0]
    x_ctx = t_in["x_prompt"][0]
    w_in_v = t_in["w_in"][0].rearrange("(j p) n -> p j n", p=P)
    w_out_v = t_in["w_out"][0].rearrange("(j p) n -> p j n", p=P)
    w_ada_v = t_in["w_ada"][0].rearrange("(j p) n -> p j n", p=P)
    w_rt_v = t_in["w_router"][0].rearrange("(j p) n -> p j n", p=P)

    def spread(row, n=P):
        return row.rearrange("(o n) -> o n", o=1).broadcast_to([n, row.shape[0]])

    ctx = ExitStack()
    with ctx:
        W = 53200
        AR = ctx.enter_context(nc.sbuf_tensor("arena", [P, W], F32))
        PS = ctx.enter_context(nc.psum_tensor("psum", [P, 8 * H], F32))
        sems = {}

        def sem(name):
            if name not in sems:
                sems[name] = nc.alloc_semaphore(name=name)
            return sems[name]

        @contextmanager
        def stage(keep):
            with nc.Block() as block:
                yield block
            done = [n for n in sems if n not in keep.split() + ["ident_in"]]
            with nc.Block() as clear:
                @clear.sync
                def _(sp):
                    for n in done:
                        sp.sem_clear(sems[n])
            for n in done:
                nc.release_semaphore(sems.pop(n))

        def ar(at, n, rows=P, r0=0):
            assert at + n <= W
            return AR[r0:r0 + rows, at:at + n]

        def r3(ap, a):
            return ap.rearrange("p (a b) -> p a b", a=a)

        qkT = r3(ar(0, 4 * TOK), 4)
        v_all = r3(ar(4608, NT * H), NT)
        ga_all = r3(ar(9216, NT * H), NT)
        qaT = r3(ar(13824, 4 * TOK), 4)
        kaT = ar(18432, TOK + NC * P)
        va = r3(ar(19840, (NT + NC) * P), NT + NC)
        lrT = ar(21248, TOK, 2 * RANK)
        w_in = r3(ar(22400, KT * DIN), KT)
        xs = [ar(41088 + DM * i, DM) for i in range(2)]
        hT = [ar(43136 + DM * i, DM) for i in range(2)]
        mA = [ar(45184, DM), ar(46208, DM)]
        mAc = [ar(21248, DM), ar(44160, DM)]
        xjunk = ar(47232, H).bitcast(mybir.dt.bfloat16)
        sq = ar(47744, 640)
        qks = ar(48384, 512)
        sg = ar(48896, 512)
        qn = ar(49408, 640)
        qw = ar(50048, 640)
        qr = ar(50688, 640)
        lrs = ar(51328, 32)
        rope = [ar(51360 + 128 * i, 128) for i in range(2)]
        ident = ar(51616, P)
        nw = ar(51744, 2 * HD)
        gn = ar(51872, DV)
        small = ar(52000, 680)
        so = [0]

        def sm(n, rows=P):
            so[0] += n
            return small[0:rows, so[0] - n:so[0]]

        RING_A = [r3(ar(4608 + 4096 * i, 4096), KT) for i in range(3)]
        crow = ar(0, P, 2 * KT)
        scT = ar(52936, 2 * KT)
        sgc = ar(144, 2 * KT)
        brow = ar(512, 2048, 2)
        mrow = ar(2560, 2048, 2)
        nrow = ar(16896, DM, 2)
        D = ar(22400, 4 * TOK).rearrange("p (d q t) -> p d q t", d=2, q=2)
        RING_B = [r3(ar(27008 + 4096 * i, 4096), KT) for i in range(3)]
        ab = [ar(41088 + TOK * i, TOK) for i in range(2)]
        lg = [ar(43392 + TOK * i, TOK) for i in range(2)]
        pre = ar(45696, TOK)
        keep = ar(46848, TOK)
        brow2 = [ar(48000 + 1536 * i, H, 2) for i in range(2)]
        mrow2 = [ar(48512 + 1536 * i, H, 2) for i in range(2)]
        nrow2 = [ar(49024 + 1536 * i, H, 2) for i in range(2)]
        ek = ar(41088, H)
        kf = ar(41600, H)
        kTM = ar(42112, H)
        U = ar(42624, NT * H).rearrange("p (g u c) -> p g u c", g=NT, u=4)
        S = r3(ar(36224, H), 4)
        St = r3(ar(36736, H), 4)
        seen = ar(37248, H).bitcast(I32)
        Sb = ar(27008, NT * 2 * H).rearrange("p (g u h c) -> p g u h c", g=NT, u=4, h=2)
        eq = ar(41088, H)
        ekc = ar(41600, H)
        qf = ar(42112, H)
        kfc = ar(42624, H)
        sc = [ar(43136 + H * i, H) for i in range(2)]
        osq = ar(44160, H)
        on = ar(44672, H)
        oatt = r3(ar(36224, NT * H), NT)
        qst = ar(45184, H)
        pr = [ar(45696 + KEYS * i, KEYS) for i in range(2)]
        pT = [ar(48256 + KEYS * i, KEYS) for i in range(2)]
        kc = r3(ar(50816, NC * P), NC)
        w_out = r3(ar(27008, KT * DM), KT)
        mE = [[ar(3 * DM * c + DM * i, DM) for i in range(3)] for c in range(2)]
        xr = ar(41472, DM)
        mixs = ar(42496, DM)
        x1 = ar(43520, DM)
        h2 = ar(44544, DM)
        mixT = ar(45568, DM)
        h2T = ar(46592, DM)
        junkE = ar(47616, H).bitcast(mybir.dt.bfloat16)
        w_rt = r3(ar(48128, KT * NE), KT)
        zeros = ar(49984, DM)
        spares = r3(ar(51072, TOPK * NE), TOPK)
        BF = mybir.dt.bfloat16
        raw = [ar(at, 4096) for at in (13824, 17920, 22016, 9728)]
        parts = [ar(26112 + 4096 * i, 4096).bitcast(BF) for i in range(CHUNKS)]
        w_hi, w_lo = [w[:, 0:4096] for w in parts], [w[:, 4096:8192] for w in parts]
        xg, xT, gw, uw, actT, yo = (ar(DM * i, DM) for i in range(6))
        act = uw
        xT_hi, xT_lo = xT.bitcast(BF)[:, 0:DM], xT.bitcast(BF)[:, DM:2 * DM]
        aT_hi, aT_lo = actT.bitcast(BF)[:, 0:DM], actT.bitcast(BF)[:, DM:2 * DM]
        sgm = ar(6 * DM, H)
        bias = ar(6 * DM + H, 3 * DM)
        ys = [ar(DM * i, DM) for i in range(2)]
        xf = [ar(2 * DM + DM * i, DM) for i in range(2)]
        mG = [ar(4 * DM, DM), ar(5 * DM, DM)]
        fn = ar(6 * DM, DM)
        yf = [ar(7 * DM + DM * i, DM) for i in range(2)]

        WG = ar(51072, 2 * 2 * P, 2 * RANK).rearrange("p (d c) -> p d c", d=2)

        upper = ar(52680, P)
        ones = ar(52808, P)
        negh = sm(10)
        ss, msq, rstd = sm(1), sm(1), sm(1)
        ssq, vq, rq = sm(10), sm(10), sm(10)
        so4, vo4, ro4 = sm(4), sm(4), sm(4)
        vecs = sm(3 * 4 * NT).rearrange("p (k u g) -> p k u g", k=3, u=4)
        bgate = sm(4)
        mx, nmx, rs, rrs = sm(8), sm(8), sm(8), sm(8)
        top8, idxf, exg, gates = sm(8), sm(8), sm(4), sm(4)
        top8i = sm(8).bitcast(U32)
        gsum, gcp, ntop = sm(1), sm(1), sm(1)
        slotf, sloti = sm(4), sm(4).bitcast(I32)
        ent = sm(8).bitcast(I32)
        logit, brt, picked, pickedsum, place, expert, spare = (sm(NE) for _ in range(7))
        tokid = sm(NT)
        cnti, ntl, tstartf = sm(NE).bitcast(I32), sm(NE), sm(NE)
        tstart = sm(NE + 1).bitcast(I32)
        tlast = sm(NE).bitcast(I32)
        listed, held, current = sm(2).bitcast(I32), sm(2), sm(2)

        def bank(b, n=H, off=0):
            return PS[:, b * H + off:b * H + off + n]

        def bc(ap, n):
            p_, a_ = ap.shape
            return ap.unsqueeze(2).broadcast_to([p_, a_, n])

        def wait(eng, sem_, value):
            eng.wait_ge(sem_, value)
            if not isinstance(value, int):
                eng.wait_ge(sem("ident_in"), 16)

        def settle(eng, steps):
            eng.sem_inc(sem(steps), 1)

        with stage("const_set norms_in pads_out modc_in modl_in w_in_in x_in0 x_in1 rope_in1") as block:
            @block.sync
            def _(sp):
                sp.dma_start(crow[0:KT, :], t_in["c"][0].rearrange("(j p) -> j p", p=P)).then_inc(sem("cond_in"), 16)
                sp.dma_start(crow[KT:2 * KT, :], t_in["c_ctx"].rearrange("(j p) -> j p", p=P)).then_inc(sem("cond_in"), 16)
                sp.dma_start(ident, t_in["ident"]).then_inc(sem("ident_in"), 16)
                for n in range(4):
                    if n >= 3:
                        sp.wait_ge(sem("ada1_made"), n - 2)
                    sp.dma_start(RING_A[n % 3], w_ada_v[:, :, n * H:(n + 1) * H]).then_inc(sem(f"ada_in{n}"), 16)
                for j in range(KT):
                    sp.dma_start(w_in[:, j, :], w_in_v[:, j, :]).then_inc(sem("w_in_in"), 16)
                sp.wait_ge(sem("mod1_ready"), 4)
                sp.dma_start(mod_d[:, 0:2, :], mrow.rearrange("p (a b) -> p a b", a=2)).then_inc(sem("mod1_out"), 16)
                sp.wait_ge(sem("mod1_out"), 16)
                for i, r in ((0, 1), (1, 0)):
                    sp.dma_start(mAc[i], spread(mod_d[1, r])).then_inc(sem("modc_in"), 16)
                for i, r in ((0, 1), (1, 0)):
                    sp.dma_start(mA[i], spread(mod_d[0, r])).then_inc(sem("modl_in"), 16)

            @block.scalar
            def _(act):
                act.dma_start(brow, spread(t_in["b_ada"][0, 0:2048], 2)).then_inc(sem("brow_in"), 16)
                act.dma_start(nrow, spread(t_in["norm_mix"][0], 2)).then_inc(sem("brow_in"), 16)
                act.dma_start(xs[0], x_ctx).then_inc(sem("x_in0"), 16)
                act.dma_start(xs[1], x_lat[0:P, :]).then_inc(sem("x_in1"), 16)
                act.dma_start(rope[1], t_in["rope"][0:P, :]).then_inc(sem("rope_in1"), 16)
                act.dma_start(nw[:, 0:HD], spread(t_in["q_norm"][0])).then_inc(sem("norms_in"), 16)
                act.dma_start(nw[:, HD:2 * HD], spread(t_in["k_norm"][0])).then_inc(sem("norms_in"), 16)
                act.dma_start(gn, spread(t_in["gla_norm"][0])).then_inc(sem("norms_in"), 16)
                act.dma_start(upper, t_in["upper"]).then_inc(sem("norms_in"), 16)
                act.dma_start(tokid, t_in["tokid"]).then_inc(sem("norms_in"), 16)
                act.dma_start(expert, spread(t_in["expert_id"])).then_inc(sem("norms_in"), 16)
                act.dma_start(brt, spread(t_in["b_router"][0])).then_inc(sem("norms_in"), 16)
                act.dma_start(list_d.rearrange("(p a) w -> p (a w)", p=P), t_in["list_pads"].rearrange("(p a) w -> p (a w)", p=P)).then_inc(sem("pads_out"), 16)
                act.wait_ge(sem("condT_made"), 1)
                nc.scalar.activation(sgc, bank(7, 2 * KT), ACT.Sigmoid).then_inc(sem("cond_sig"), 1)

            @block.gpsimd
            def _(pool):
                nc.gpsimd.memset(negh, -0.5).then_inc(sem("const_set"), 1)
                nc.gpsimd.memset(ones, 1.0).then_inc(sem("const_set"), 1)
                nc.gpsimd.memset(pickedsum, 0.0).then_inc(sem("const_set"), 1)

            @block.vector
            def _(dve):
                dve.wait_ge(sem("cond_sig"), 1)
                nc.vector.tensor_tensor(scT, bank(7, 2 * KT), sgc, ALU.mult).then_inc(sem("scT_ready"), 1)
                dve.wait_ge(sem("brow_in"), 32)
                own = Chain(dve, sem("own_a0"))
                for n in range(4):
                    piece = mrow[:, n * H:(n + 1) * H]
                    dve.wait_ge(sem("ada1_made"), n + 1)
                    add = nc.vector.tensor_tensor(piece, bank(n)[0:2, :], brow[:, n * H:(n + 1) * H], ALU.add)
                    if n < 2:
                        add.then_inc(sem("mod1_ready"), 1)
                    else:
                        own.link(add)
                        nc.vector.scalar_tensor_tensor(piece, piece, 1.0, nrow[:, (n - 2) * H:(n - 1) * H],
                                                       ALU.add, ALU.mult).then_inc(sem("mod1_ready"), 1)

            @block.tensor
            def _(pe):
                pe.wait_ge(sem("cond_in"), 32)
                pe.wait_ge(sem("ident_in"), 16)
                nc.tensor.transpose(bank(7, 2 * KT), crow, ident[0:2 * KT, 0:2 * KT]).then_inc(sem("condT_made"), 1)
                pe.wait_ge(sem("scT_ready"), 1)
                for n in range(4):
                    pe.wait_ge(sem(f"ada_in{n}"), 16)
                    for j in range(KT):
                        last = nc.tensor.matmul(bank(n)[0:2, :], scT[:, j:2 * KT:KT], RING_A[n % 3][:, j, :],
                                                start=(j == 0), stop=(j == KT - 1))
                    last.then_inc(sem("ada1_made"), 1)

        with stage("const_set pads_out") as block:
            def tiles(eng, body):
                body(0, 0, 1, False)
                with eng.Fori(0, NS // 2) as i:
                    body(i * 2 + 1, 1, i + 1, True)
                    body(i * 2 + 2, 0, i + 2, True)

            @block.sync
            def _(sp):
                def load(g, slot, src_tile):
                    wait(sp, sem("x_transposed"), g - 1)
                    sp.dma_start(xs[slot], x_lat[ds(src_tile * P, P), :]).then_inc(sem(f"x_in{slot}"), 16)
                    wait(sp, sem("rotated"), g - 1)
                    sp.dma_start(rope[slot], t_in["rope"][ds(src_tile * P, P), :]).then_inc(sem(f"rope_in{slot}"), 16)

                sp.wait_ge(sem("rotated"), 1)
                sp.wait_ge(sem("va_kept"), 1)
                sp.dma_start(t_out["new_k"][0, 0].rearrange("s h d -> s (h d)"), qr[:, H:H + P]).then_inc(sem("out_kv"), 16)
                sp.dma_start(t_out["new_v"][0, 0].rearrange("s h d -> s (h d)"), va[:, 0, :]).then_inc(sem("out_kv"), 16)
                with sp.Fori(0, NS // 2 - 1) as i:
                    load(i * 2 + 2, 0, i * 2 + 1)
                    load(i * 2 + 3, 1, i * 2 + 2)
                load(NS, 0, NS - 1)
                sp.wait_ge(sem("x_transposed"), NS)
                sp.dma_start(xs[1], x_lat[0:P, :]).then_inc(sem("x_in1"), 16)

            @block.scalar
            def _(act):
                act.wait_ge(sem("x_in0"), 16)
                nc.scalar.activation(xjunk, xs[0], ACT.Square, accum_out=ss).then_inc(sem("x_squared"), 1)
                def body(g, b, n, latent):
                    nb, nn = 1 - b, (n if b == 0 else n + 1)
                    wait(act, sem(f"x_in{nb}"), nn * 16)
                    wait(act, sem("x_normed"), g + 1)
                    nc.scalar.activation(xjunk, xs[nb], ACT.Square, accum_out=ss).then_inc(sem("x_squared"), 1)
                    wait(act, sem("proj_qb"), g + 1)
                    wait(act, sem("rotated"), g)
                    nc.scalar.activation(sq[:, 0:H], bank(2), ACT.Square).then_inc(sem("qb_squared"), 1)
                    wait(act, sem("proj_kv"), g + 1)
                    wait(act, sem("lr_transposed"), g)
                    nc.scalar.activation(lrs, bank(3, 32), ACT.Copy).then_inc(sem("lr_staged"), 1)
                    nc.scalar.activation(va[:, ds(g, 1), :], bank(3, P, 32 + P).unsqueeze(1), ACT.Copy).then_inc(sem("va_kept"), 1)
                    nc.scalar.activation(sq[:, H:H + P], bank(3, P, 32), ACT.Square).then_inc(sem("kb_squared"), 1)
                    wait(act, sem("x_transposed"), g + 2)
                    wait(act, sem("proj_ga"), g)
                    nc.scalar.activation(hT[nb], PS[:, 0:DM], ACT.Copy).then_inc(sem("hT_ready"), 1)
                    wait(act, sem("proj_qk"), g + 1)
                    wait(act, sem("qk_transposed"), g)
                    nc.scalar.activation(qks, bank(4), ACT.Copy).then_inc(sem("qk_staged"), 1)
                    wait(act, sem("qk_transposed"), g + 1)
                    nc.scalar.activation(qkT[:, :, ds(g * P, P)], r3(bank(7), 4), ACT.Copy).then_inc(sem("qkT_kept"), 1)
                    wait(act, sem("proj_ga"), g + 1)
                    wait(act, sem("ga_kept"), g)
                    nc.scalar.activation(sg, bank(6), ACT.Sigmoid).then_inc(sem("ga_sig"), 1)
                    wait(act, sem("lr_transposed"), g + 1)
                    nc.scalar.activation(kaT[:, ds(g * P, P)], bank(7, P), ACT.Copy)
                    nc.scalar.activation(lrT[:, ds(g * P, P)], PS[0:32, 7 * H + P:7 * H + 2 * P], ACT.Copy).then_inc(sem("lrT_kept"), 1)

                act.wait_ge(sem("x_transposed"), 1)
                nc.scalar.activation(hT[0], PS[:, 0:DM], ACT.Copy).then_inc(sem("hT_ready"), 1)
                tiles(act, body)

            @block.gpsimd
            def _(pool):
                pool.wait_ge(sem("norms_in"), 16 * 7)
                pool.wait_ge(sem("const_set"), 3)

                def norm_x(n):
                    wait(pool, sem("x_mean"), n)
                    nc.gpsimd.tensor_tensor(rstd, msq, negh[:, 0:1], ALU.pow).then_inc(sem("x_rstd"), 1)

                norm_x(1)
                def body(g, b, n, latent):
                    norm_x(g + 2)
                    wait(pool, sem("qk_mean"), g + 1)
                    nc.gpsimd.tensor_tensor(rq, vq, negh, ALU.pow).then_inc(sem("qk_rstd"), 1)
                    wait(pool, sem("qk_scaled"), g + 1)
                    wait(pool, sem("rotated"), g)
                    for lo, m, half in ((0, NH, 0), (H, NKV, 1)):
                        nc.gpsimd.tensor_tensor(r3(qw[:, lo:lo + m * HD], m), r3(qn[:, lo:lo + m * HD], m),
                                                nw[:, half * HD:half * HD + HD].unsqueeze(1).broadcast_to([P, m, HD]),
                                                ALU.mult).then_inc(sem("qk_weighted"), 1)
                    if latent:
                        wait(pool, sem("qk_weighted"), g * 2 + 2)
                        wait(pool, sem(f"rope_in{b}"), (n if b else n - 1) * 16)
                        S2 = rope[b][:, HD:2 * HD]
                        pairs = lambda ap, o: ap.rearrange("p (h c two) -> p h c two", h=NH + NKV, two=2)[:, :, :, o]
                        for o in range(2):
                            nc.gpsimd.tensor_tensor(pairs(qn, o), pairs(qw, 1 - o),
                                                    S2.rearrange("p (c two) -> p c two", two=2)[:, :, o].unsqueeze(1)
                                                    .broadcast_to([P, NH + NKV, HD // 2]),
                                                    ALU.mult).then_inc(sem("swapped"), 1)
                    wait(pool, sem("ga_kept"), g + 1)
                    gg = ga_all[:, ds(g, 1), :].rearrange("p a (h c) -> p (a h) c", h=GH)
                    nc.gpsimd.tensor_tensor(gg, gg, gn.unsqueeze(1).broadcast_to([P, GH, DV]), ALU.mult).then_inc(sem("ga_done"), 1)

                tiles(pool, body)

            @block.vector
            def _(dve):
                own = Chain(dve, sem("own_a"))
                own.start(0)
                dve.wait_ge(sem("modc_in"), 32)
                dve.wait_ge(sem("modl_in"), 32)

                def norm_x(g, slot, nload, mods):
                    wait(dve, sem("x_squared"), g + 1)
                    nc.vector.tensor_scalar(msq, ss, 1.0 / DM, EPS, ALU.mult, ALU.add).then_inc(sem("x_mean"), 1)
                    wait(dve, sem("x_rstd"), g + 1)
                    own.link(nc.vector.scalar_tensor_tensor(xs[slot], xs[slot], rstd, mods[0], ALU.mult, ALU.mult))
                    nc.vector.tensor_tensor(xs[slot], xs[slot], mods[1], ALU.add).then_inc(sem("x_normed"), 1)

                def by_head(ap, order):
                    return ap[:, 0:H].rearrange(f"p ({order} c) -> p v r c", v=NKV, r=NH // NKV)

                norm_x(0, 0, 1, mAc)
                def body(g, b, n, latent):
                    own.start(g * 3 if latent else 1)
                    norm_x(g + 1, 1 - b, None, mA)
                    wait(dve, sem("kb_squared"), g + 1)
                    own.link(nc.vector.tensor_reduce(ssq, r3(sq, NH + NKV), AX.X, ALU.add))
                    nc.vector.tensor_scalar(vq, ssq, 1.0 / HD, EPS, ALU.mult, ALU.add).then_inc(sem("qk_mean"), 1)
                    wait(dve, sem("qk_rstd"), g + 1)
                    nc.vector.tensor_tensor(r3(qn[:, 0:H], NH), r3(bank(2), NH), bc(rq[:, 0:NH], HD), ALU.mult).then_inc(sem("q_scaled"), 1)
                    nc.vector.tensor_tensor(r3(qn[:, H:H + P], NKV), r3(bank(3, P, 32), NKV), bc(rq[:, NH:NH + NKV], HD),
                                            ALU.mult).then_inc(sem("qk_scaled"), 1)
                    if latent:
                        C2 = rope[b][:, 0:HD]
                        wait(dve, sem("qk_weighted"), g * 2 + 2)
                        wait(dve, sem(f"rope_in{b}"), (n if b else n - 1) * 16)
                        own.link(nc.vector.tensor_tensor(r3(sq, NH + NKV), r3(qw, NH + NKV),
                                                         C2.unsqueeze(1).broadcast_to([P, NH + NKV, HD]), ALU.mult))
                        wait(dve, sem("swapped"), g * 2)
                        wait(dve, sem("lr_transposed"), g)
                        dve.wait_ge(sem("out_kv"), 32)
                        nc.vector.tensor_tensor(by_head(qr, "r v"), by_head(sq, "v r"), by_head(qn, "v r"), ALU.add)
                        nc.vector.tensor_tensor(qr[:, H:H + P], sq[:, H:H + P], qn[:, H:H + P], ALU.add).then_inc(sem("rotated"), 1)
                    else:
                        dve.wait_ge(sem("qk_weighted"), 2)
                        nc.vector.tensor_copy(by_head(qr, "r v"), by_head(qw, "v r"))
                        nc.vector.tensor_copy(qr[:, H:H + P], qw[:, H:H + P]).then_inc(sem("rotated"), 1)
                    wait(dve, sem("qa_transposed"), g + 1)
                    nc.vector.tensor_copy(qaT[:, :, ds(g * P, P)], r3(bank(7), 4)).then_inc(sem("qaT_kept"), 1)
                    wait(dve, sem("proj_va"), g + 1)
                    nc.vector.tensor_copy(v_all[:, ds(g, 1), :], bank(5).unsqueeze(1)).then_inc(sem("v_kept"), 1)
                    wait(dve, sem("ga_sig"), g + 1)
                    nc.vector.tensor_tensor(ga_all[:, ds(g, 1), :], bank(6).unsqueeze(1), sg.unsqueeze(1), ALU.mult).then_inc(sem("ga_kept"), 1)

                tiles(dve, body)

            @block.tensor
            def _(pe):
                def x_transpose(g, slot):
                    wait(pe, sem("x_normed"), g + 1)
                    wait(pe, sem("hT_ready"), g)
                    for j in range(KT):
                        last = nc.tensor.transpose(PS[:, j * P:(j + 1) * P], xs[slot][:, j * P:(j + 1) * P], ident)
                    last.then_inc(sem("x_transposed"), 1)

                def project(b, bk, off, lo, n, done):
                    for j in range(KT):
                        last = nc.tensor.matmul(bank(bk, n, off), hT[b][:, j * P:(j + 1) * P], w_in[:, j, lo:lo + n],
                                                start=(j == 0), stop=(j == KT - 1))
                    if done:
                        last.then_inc(sem(done), 1)

                x_transpose(0, 0)
                pe.wait_ge(sem("w_in_in"), 16 * KT)

                def body(g, b, n, latent):
                    wait(pe, sem("hT_ready"), g + 1)
                    wait(pe, sem("qk_scaled"), g)
                    project(b, 2, 0, C_QB, H, "proj_qb")
                    project(b, 3, 0, C_LR, 32, None)
                    project(b, 3, 32, C_KB, 2 * P, "proj_kv")
                    x_transpose(g + 1, 1 - b)
                    wait(pe, sem("qk_staged"), g)
                    project(b, 4, 0, 0, H, "proj_qk")
                    wait(pe, sem("rotated"), g + 1)
                    wait(pe, sem("lrT_kept"), g)
                    for r in range(4):
                        last = nc.tensor.transpose(bank(7, P, r * P), qr[:, r * P:(r + 1) * P], ident)
                    last.then_inc(sem("qa_transposed"), 1)
                    wait(pe, sem("v_kept"), g)
                    project(b, 5, 0, 512, H, "proj_va")
                    wait(pe, sem("qk_staged"), g + 1)
                    wait(pe, sem("qaT_kept"), g + 1)
                    for r in range(4):
                        last = nc.tensor.transpose(bank(7, P, r * P), qks[:, r * P:(r + 1) * P], ident)
                    last.then_inc(sem("qk_transposed"), 1)
                    wait(pe, sem("ga_kept"), g)
                    project(b, 6, 0, 1024, H, "proj_ga")
                    wait(pe, sem("lr_staged"), g + 1)
                    wait(pe, sem("qkT_kept"), g + 1)
                    nc.tensor.transpose(bank(7, P), qr[:, H:H + P], ident)
                    nc.tensor.transpose(PS[0:32, 7 * H + P:7 * H + 2 * P], lrs, ident).then_inc(sem("lr_transposed"), 1)

                tiles(pe, body)

        NADA = 8
        with stage("pads_out state_in vecs_ready seen_in") as block:
            @block.sync
            def _(sp):
                sp.wait_ge(sem("const_set"), 4)
                sp.dma_start(WG[0:RANK, 0, :], t_in["w_gate_f"][0]).then_inc(sem("gate_w_in"), 16)
                sp.dma_start(WG[RANK:2 * RANK, 1, :], t_in["w_gate_b"][0]).then_inc(sem("gate_w_in"), 16)
                for d, name in enumerate(("b_gate_f", "b_gate_b")):
                    for q in range(2):
                        sp.dma_start(bgate[:, 2 * d + q:2 * d + q + 1],
                                     t_in[name][0, q * P:(q + 1) * P].rearrange("(p o) -> p o", o=1)).then_inc(sem("gate_b_in"), 16)
                sp.dma_start(keep, spread(t_in["keep"])).then_inc(sem("keep_in"), 16)
                for n in range(NADA):
                    if n >= 3:
                        sp.wait_ge(sem("ada2_made"), n - 2)
                    sp.dma_start(RING_B[n % 3], w_ada_v[:, :, (n + 4) * H:(n + 5) * H]).then_inc(sem(f"ada2_in{n % 3}"), 16)
                    if n >= 2:
                        sp.wait_ge(sem("mod2_ready"), n - 1)
                    sp.dma_start(brow2[n % 2], spread(t_in["b_ada"][0, (n + 4) * H:(n + 5) * H], 2)).then_inc(sem(f"brow2_in{n % 2}"), 16)
                    if n in (4, 5):
                        sp.dma_start(nrow2[n % 2], spread(t_in["norm_ffn"][0, (n - 4) * H:(n - 3) * H], 2)).then_inc(sem("nrow2_in"), 16)
                sp.wait_ge(sem("ada2_made"), NADA - 2)
                sp.dma_start(seen, t_in["seen"]).then_inc(sem("seen_in"), 16)
                for d, name in enumerate(("state_gla_fwd", "state_gla_bwd")):
                    for half in range(2):
                        sp.dma_start(S[64 * half:64 * half + 64, 2 * d:2 * d + 2, :],
                                     t_in[name][0, 0].rearrange("(q h) k v -> h k q v", h=2)[half]).then_inc(sem("state_in"), 16)

            @block.scalar
            def _(act):
                own = Chain(act, sem("own_b1_act"))
                act.wait_ge(sem("gate_b_in"), 64)
                for u in range(4):
                    z = PS[:, (u % 2) * 3 * H:(u % 2) * 3 * H + 3 * H].rearrange("p (a b) -> p a b", a=3)[:, :, 0:384]
                    a = ab[u % 2]
                    act.wait_ge(sem("z_made"), u + 1)
                    if u >= 2:
                        act.wait_ge(sem("decay_logged"), u - 1)
                    nc.scalar.activation(r3(a, 3), z, ACT.Abs, bias=bgate[:, u:u + 1]).then_inc(sem("abs_made"), 1)
                    act.wait_ge(sem("abs_made"), u + 1)
                    own.link(nc.scalar.activation(a, a, ACT.Exp, scale=-1.0))
                    nc.scalar.activation(a, a, ACT.Ln, bias=1.0).then_inc(sem("ln_made"), 1)
                act.wait_ge(sem("vecs_raw"), 4)
                flat = vecs.rearrange("p k u g -> p (k u g)")
                nc.scalar.activation(flat, flat, ACT.Exp, scale=1.0 / 16).then_inc(sem("vecs_ready"), 1)

            @block.gpsimd
            def _(pool):
                nc.gpsimd.memset(ar(51072, 2 * 2 * P, 2 * RANK), 0.0).then_inc(sem("const_set"), 1)
                for n in range(NADA):
                    pool.wait_ge(sem("mod2_ready"), n + 1)
                    pool.dma_start(mod_d[:, 2 + n // 2, (n % 2) * H:(n % 2 + 1) * H], mrow2[n % 2]).then_inc(sem(f"mod2_out{n % 2}"), 16)
                pool.wait_ge(sem("mod2_out0"), 16 * NADA // 2)
                pool.wait_ge(sem("mod2_out1"), 16 * NADA // 2)

            @block.vector
            def _(dve):
                own = Chain(dve, sem("own_b1"))
                dve.wait_ge(sem("keep_in"), 16)

                def decay(u):
                    d = u // 2
                    z = PS[:, (u % 2) * 3 * H:(u % 2) * 3 * H + 3 * H].rearrange("p (a b) -> p a b", a=3)[:, :, 0:384]
                    l = lg[u % 2]
                    dve.wait_ge(sem("abs_made"), u + 1)
                    nc.vector.tensor_scalar(r3(l, 3), z, bgate[:, u:u + 1], 0.0, ALU.add, ALU.min).then_inc(sem("z_read"), 1)
                    dve.wait_ge(sem("z_read"), u + 1)
                    dve.wait_ge(sem("ln_made"), u + 1)
                    nc.vector.tensor_tensor(l, l, ab[u % 2], ALU.subtract).then_inc(sem("decay_logged"), 1)
                    dve.wait_ge(sem("decay_logged"), u + 1)
                    own.link(nc.vector.tensor_tensor_scan(pre, keep, l, 0.0, ALU.mult, ALU.add))
                    p3, l3, D3 = r3(pre, NT), r3(l, NT), D[:, d, u % 2, :].rearrange("p (g t) -> p g t", g=NT)
                    whole, update, centre = (vecs[:, k, u, :] for k in range(3))
                    last, mid = p3[:, :, P - 1:P].rearrange("p g o -> p (g o)"), P // 2
                    if d == 0:
                        c = p3[:, :, mid - 1:mid].rearrange("p g o -> p (g o)")
                        nc.vector.tensor_tensor(D3, p3, bc(c, P), ALU.subtract)
                        nc.vector.tensor_copy(whole, last)
                        nc.vector.tensor_copy(centre, c)
                        nc.vector.tensor_tensor(update, last, c, ALU.subtract).then_inc(sem("vecs_raw"), 1)
                    else:
                        own.link(nc.vector.tensor_tensor(l, pre, l, ALU.subtract))
                        c = l3[:, :, mid:mid + 1].rearrange("p g o -> p (g o)")
                        nc.vector.tensor_tensor(D3, bc(c, P), l3, ALU.subtract)
                        nc.vector.tensor_copy(whole, last)
                        nc.vector.tensor_copy(update, c)
                        nc.vector.tensor_tensor(centre, last, c, ALU.subtract).then_inc(sem("vecs_raw"), 1)

                def ada(n):
                    to = mrow2[n % 2]
                    dve.wait_ge(sem(f"brow2_in{n % 2}"), 16 * (n // 2 + 1))
                    dve.wait_ge(sem("ada2_made"), n + 1)
                    if n >= 2:
                        dve.wait_ge(sem(f"mod2_out{n % 2}"), 16 * (n // 2))
                    add = nc.vector.tensor_tensor(to, bank(6 + n % 2)[0:2, :], brow2[n % 2], ALU.add)
                    if n in (4, 5):
                        own.link(add)
                        dve.wait_ge(sem("nrow2_in"), 32)
                        add = nc.vector.scalar_tensor_tensor(to, to, 1.0, nrow2[n % 2], ALU.add, ALU.mult)
                    add.then_inc(sem("mod2_ready"), 1)

                for u in range(4):
                    decay(u)
                    ada(2 * u)
                    ada(2 * u + 1)

            @block.tensor
            def _(pe):
                pe.wait_ge(sem("gate_w_in"), 32)

                def gates(u):
                    if u >= 2:
                        pe.wait_ge(sem("z_read"), u - 1)
                    for a in range(3):
                        last = nc.tensor.matmul(bank((u % 2) * 3 + a, 384), WG[:, u // 2, (u % 2) * P:(u % 2 + 1) * P],
                                                lrT[:, a * 384:(a + 1) * 384], start=True, stop=True)
                    last.then_inc(sem("z_made"), 1)

                def ada(n):
                    pe.wait_ge(sem(f"ada2_in{n % 3}"), 16 * (n // 3 + 1))
                    if n >= 2:
                        pe.wait_ge(sem("mod2_ready"), n - 1)
                    for j in range(KT):
                        last = nc.tensor.matmul(bank(6 + n % 2)[0:2, :], scT[:, j:2 * KT:KT], RING_B[n % 3][:, j, :],
                                                start=(j == 0), stop=(j == KT - 1))
                    last.then_inc(sem("ada2_made"), 1)

                gates(0)
                gates(1)
                for u in range(4):
                    ada(2 * u)
                    if u < 2:
                        gates(u + 2)
                    ada(2 * u + 1)

        with stage("pads_out seen_in") as block:
            kT_tile = lambda g: qkT[:, 2:4, ds(g * P, P)].unsqueeze(1).broadcast_to([P, 2, 2, P])
            D_tile = lambda g: D[:, :, :, ds(g * P, P)]
            r4 = lambda ap: ap.rearrange("p (d q t) -> p d q t", d=2, q=2)

            @block.sync
            def _(sp):
                sp.wait_ge(sem("added"), 1)
                for d, name in enumerate(("new_sf", "new_sb")):
                    for half in range(2):
                        sp.dma_start(t_out[name][0, 0].rearrange("(q h) k v -> h k q v", h=2)[half],
                                     U[64 * half:64 * half + 64, 0, 2 * d:2 * d + 2, :]).then_inc(sem("out_states"), 16)
                sp.wait_ge(sem("out_states"), 64)

            @block.scalar
            def _(act):
                def grow(g):
                    nc.scalar.activation(r4(ek), D_tile(g), ACT.Exp, scale=-1.0 / 16).then_inc(sem("ek_made"), 1)

                def keep_turned(g):
                    wait(act, sem("kf_transposed"), g + 1)
                    wait(act, sem("sums_made"), g)
                    nc.scalar.activation(kTM, bank(0), ACT.Copy).then_inc(sem("kTM_made"), 1)

                grow(0)
                with act.Fori(0, NT - 1) as g:
                    wait(act, sem("kf_made"), g + 1)
                    grow(g + 1)
                    keep_turned(g)
                keep_turned(NT - 1)

            @block.gpsimd
            def _(pool):
                nc.gpsimd.memset(ar(27008, NT * 2 * H), 0.0).then_inc(sem("Sb_cleared"), 1)
                pool.wait_ge(sem("state_in"), 64)
                pool.wait_ge(sem("vecs_ready"), 1)
                pool.wait_ge(sem("Sb_cleared"), 1)
                with pool.Fori(0, NS) as i:
                    wait(pool, sem("stepped"), i)
                    for d, g in enumerate((i + 1, NS - i)):
                        for half in range(2):
                            rows = slice(64 * half, 64 * half + 64)
                            us = slice(2 * d, 2 * d + 2)
                            nc.gpsimd.tensor_tensor(Sb[rows, ds(g, 1), us, half, :].rearrange("p o u c -> p (o u) c"),
                                                    S[rows, us, :],
                                                    vecs[rows, 2, us, ds(g, 1)].broadcast_to([64, 2, P]),
                                                    ALU.mult).then_inc(sem("state_kept"), 1)

            @block.vector
            def _(dve):
                own = Chain(dve, sem("own_b2"))
                dve.wait_ge(sem("vecs_ready"), 1)
                def decay_keys(g):
                    wait(dve, sem("ek_made"), g + 1)
                    wait(dve, sem("kf_transposed"), g)
                    nc.vector.tensor_tensor(r4(kf), kT_tile(g), r4(ek), ALU.mult).then_inc(sem("kf_made"), 1)

                def keep_sums(g):
                    wait(dve, sem("sums_made"), g + 1)
                    for half in range(2):
                        rows = slice(64 * half, 64 * half + 64)
                        last = nc.vector.tensor_tensor(U[rows, ds(g, 1), :, :].rearrange("p o u c -> p (o u) c"),
                                                       PS[rows, H:3 * H].rearrange("p (u h c) -> p u h c", u=4, h=2)[:, :, half, :],
                                                       vecs[rows, 1, :, ds(g, 1)].broadcast_to([64, 4, P]), ALU.mult)
                    last.then_inc(sem("added"), 1)

                decay_keys(0)
                with dve.Fori(0, NT - 1) as g:
                    decay_keys(g + 1)
                    keep_sums(g)
                keep_sums(NT - 1)
                dve.wait_ge(sem("added"), NT)
                dve.wait_ge(sem("state_in"), 64)
                with dve.Fori(0, NS) as i:
                    own.start(i)
                    for d, g in enumerate((i + 1, NS - i)):
                        us = slice(2 * d, 2 * d + 2)
                        last = nc.vector.tensor_tensor(St[:, us, :], S[:, us, :], vecs[:, 0, us, ds(g, 1)].broadcast_to([P, 2, P]), ALU.mult)
                    own.link(last)
                    wait(dve, sem("state_kept"), i * 4 + 4)
                    for d, g in enumerate((i + 1, NS - i)):
                        us = slice(2 * d, 2 * d + 2)
                        last = nc.vector.tensor_tensor(S[:, us, :], St[:, us, :],
                                                       U[:, ds(g, 1), us, :].rearrange("p o u c -> p (o u) c"), ALU.add)
                    last.then_inc(sem("stepped"), 1)
                    wait(dve, sem("stepped"), i + 1)

            @block.tensor
            def _(pe):
                def turn(g):
                    wait(pe, sem("kf_made"), g + 1)
                    wait(pe, sem("kTM_made"), g)
                    for u in range(4):
                        last = nc.tensor.transpose(bank(0, P, u * P), kf[:, u * P:(u + 1) * P], ident)
                    last.then_inc(sem("kf_transposed"), 1)

                def add(g):
                    wait(pe, sem("kTM_made"), g + 1)
                    wait(pe, sem("added"), g)
                    for u in range(4):
                        q = u % 2
                        last = nc.tensor.matmul(bank(1 + u // 2, 2 * P, q * 2 * P), kTM[:, u * P:(u + 1) * P],
                                                v_all[:, ds(g, 1), q * 2 * DV:(q + 1) * 2 * DV].rearrange("p o c -> p (o c)"),
                                                start=True, stop=True)
                    last.then_inc(sem("sums_made"), 1)

                turn(0)
                with pe.Fori(0, NT - 1) as g:
                    turn(g + 1)
                    add(g)
                add(NT - 1)

        with stage("pads_out") as block:
            @block.scalar
            def _(act):
                def grow(g):
                    wait(act, sem("qk_decayed"), g)
                    nc.scalar.activation(r4(eq), D_tile(g), ACT.Exp, scale=1.0 / 16).then_inc(sem("eq_made"), 1)
                    nc.scalar.activation(r4(ekc), D_tile(g), ACT.Exp, scale=-1.0 / 16).then_inc(sem("ekc_made"), 1)

                def square(g):
                    wait(act, sem("gla_made"), g + 1)
                    wait(act, sem("osq_read"), g)
                    nc.scalar.activation(osq.rearrange("p (a b) -> p a b", a=2),
                                         PS[:, 2 * H:4 * H].rearrange("p (a b) -> p a b", a=2)[:, :, 0:2 * P],
                                         ACT.Square).then_inc(sem("o_squared"), 1)

                grow(0)
                with act.Fori(0, NT - 1) as g:
                    grow(g + 1)
                    square(g)
                square(NT - 1)

            @block.gpsimd
            def _(pool):
                for half in range(2):
                    nc.gpsimd.memset(sc[half], 0.0).then_inc(sem("sc_cleared"), 1)
                with pool.Fori(0, NT) as g:
                    wait(pool, sem("o_mean"), g + 1)
                    nc.gpsimd.tensor_tensor(ro4, vo4, negh[:, 0:4], ALU.pow).then_inc(sem("o_rstd"), 1)

            @block.vector
            def _(dve):
                own = Chain(dve, sem("own_c"))
                dve.wait_ge(sem("sc_cleared"), 2)
                dve.wait_ge(sem("seen_in"), 16)

                def decay(g):
                    wait(dve, sem("ekc_made"), g + 1)
                    wait(dve, sem("gla_made"), g)
                    for d in range(2):
                        nc.vector.scalar_tensor_tensor(r4(qf)[:, d], qkT[:, 0:2, ds(g * P, P)], float(HD) ** -0.5, r4(eq)[:, d],
                                                       ALU.mult, ALU.mult)
                    nc.vector.tensor_tensor(r4(kfc), kT_tile(g), r4(ekc), ALU.mult).then_inc(sem("qk_decayed"), 1)

                def mask(g):
                    wait(dve, sem("gla_scored"), g + 1)
                    nc.vector.tensor_copy(spare[:, 0:1], ones[:, 0:1])
                    for half in range(2):
                        nc.vector.copy_predicated(sc[half], seen, bank(half)).then_inc(sem("gla_masked"), 1)

                def gated(g):
                    own.start(g)
                    wait(dve, sem("o_squared"), g + 1)
                    nc.vector.tensor_reduce(so4, r3(osq, GH), AX.X, ALU.add).then_inc(sem("osq_read"), 1)
                    wait(dve, sem("osq_read"), g + 1)
                    nc.vector.tensor_scalar(vo4, so4, 1.0 / DV, EPS, ALU.mult, ALU.add).then_inc(sem("o_mean"), 1)
                    wait(dve, sem("o_rstd"), g + 1)
                    own.link(nc.vector.tensor_tensor(on.rearrange("p (a b c) -> p a b c", a=2, b=2),
                                                     PS[:, 2 * H:4 * H].rearrange("p (a b c) -> p a b c", a=2, b=4)[:, :, 0:2, :],
                                                     ro4.rearrange("p (a b) -> p a b", a=2).unsqueeze(3).broadcast_to([P, 2, 2, P]), ALU.mult))
                    gg = ga_all[:, ds(g, 1), :].rearrange("p o c -> p (o c)")
                    nc.vector.tensor_tensor(gg, on, gg, ALU.mult).then_inc(sem("gla_done"), 1)

                decay(0)
                mask(0)
                with dve.Fori(0, NT - 1) as g:
                    decay(g + 1)
                    gated(g)
                    mask(g + 1)
                gated(NT - 1)

            @block.tensor
            def _(pe):
                def score(g):
                    wait(pe, sem("qk_decayed"), g + 1)
                    wait(pe, sem("gla_masked"), g * 2)
                    for half in range(2):
                        rows = slice(64 * half, 64 * half + 64)
                        for u in range(4):
                            last = nc.tensor.matmul(bank(half, P, u * P), kfc[rows, u * P:(u + 1) * P], qf[rows, u * P:(u + 1) * P],
                                                    start=True, stop=True)
                    last.then_inc(sem("gla_scored"), 1)

                def mix(g):
                    wait(pe, sem("gla_done"), g)
                    wait(pe, sem("gla_masked"), g * 2 + 2)
                    for q in range(2):
                        out = bank(2 + q, 2 * P)
                        for d in range(2):
                            u = 2 * d + q
                            nc.tensor.matmul(out, qf[:, u * P:(u + 1) * P],
                                             Sb[:, ds(g, 1), u, :, :].rearrange("p o h c -> p (o h c)"), start=(d == 0), stop=False)
                        for half in range(2):
                            h = 2 * q + half
                            for d in range(2):
                                u = 2 * d + q
                                last = nc.tensor.matmul(bank(2 + q, P, half * P), sc[half][:, u * P:(u + 1) * P],
                                                        v_all[:, ds(g, 1), h * DV:(h + 1) * DV].rearrange("p o c -> p (o c)"),
                                                        start=False, stop=(half == 1 and d == 1))
                    last.then_inc(sem("gla_made"), 1)

                score(0)
                with pe.Fori(0, NT - 1) as g:
                    mix(g)
                    score(g + 1)
                mix(NT - 1)

        SCALE = float(HD) ** -0.5
        RG = NH // NKV
        AHEAD = 2
        head = lambda hh: (hh // RG, hh % RG)
        with stage("pads_out mE_in w_out_in") as block:
            @block.sync
            def _(sp):
                for a in range(NC):
                    sp.dma_start(kc[:, a, :], t_in["cache_k"][0, 0, a * P:(a + 1) * P].rearrange("s h d -> s (h d)")).then_inc(sem("cache_in"), 16)
                    sp.dma_start(va[:, NT + a, :], t_in["cache_v"][0, 0, a * P:(a + 1) * P].rearrange("s h d -> s (h d)")).then_inc(sem("cache_in"), 16)
                for c in range(2):
                    for i, r in enumerate((2, 4, 3)):
                        sp.dma_start(mE[c][i], spread(mod_d[c, r])).then_inc(sem("mE_in"), 16)
                for j in range(KT):
                    sp.dma_start(w_out[:, j, :], w_out_v[:, j, :]).then_inc(sem("w_out_in"), 16)

            @block.gpsimd
            def _(pool):
                def q_slices(g, n):
                    for r in range(RG):
                        if n is not None:
                            wait(pool, sem("scored"), n + RG + r + 1)
                        nc.gpsimd.tensor_copy(qst[:, r * P:(r + 1) * P], qaT[:, r, ds(g * P, P)]).then_inc(sem("q_staged"), 1)

                q_slices(1, None)
                with pool.Fori(2, NT) as g:
                    q_slices(g, g * NH - 2 * NH)
                for r in range(AHEAD):
                    pool.wait_ge(sem("scored"), (NS - 1) * NH + RG + r + 1)
                    pool.sem_inc(sem("q_staged"), 1)

            @block.scalar
            def _(act):
                act.wait_ge(sem("kcT_made"), 1)
                nc.scalar.activation(kaT[:, TOK:TOK + NC * P], bank(7, NC * P), ACT.Copy).then_inc(sem("kcT_kept"), 1)
                act.wait_ge(sem("c_shifted"), 1)
                nc.scalar.activation(pr[0][:, 0:NH * P], pr[0][:, 0:NH * P], ACT.Exp, scale=SCALE).then_inc(sem("c_exp"), 1)
                act.wait_ge(sem("c_transposed"), 1)
                nc.scalar.activation(pT[0][:, 0:NH * P], PS[:, 2 * H:4 * H], ACT.Copy).then_inc(sem("c_pT"), 1)

                act.wait_ge(sem("max_made"), 1)
                nc.scalar.activation(pr[0], PS[:, 0:KEYS], ACT.Exp, bias=nmx[:, 0:1], scale=SCALE,
                                     accum_out=rs[:, 0:1]).then_inc(sem("exp_made"), 1)
                with act.Fori(0, NS) as t:
                    for hh in range(NH):
                        n = t * NH + hh
                        nx = (hh + 1) % NH
                        wait(act, sem("p_transposed"), n * 3 + 1)
                        nc.scalar.activation(pT[hh % 2][:, 0:H], bank(6), ACT.Copy).then_inc(sem("pT_first"), 1)
                        wait(act, sem("max_made"), n + 2)
                        nc.scalar.activation(pr[nx % 2], PS[:, (nx % 2) * 3 * H:(nx % 2) * 3 * H + KEYS], ACT.Exp,
                                             bias=nmx[:, nx:nx + 1], scale=SCALE, accum_out=rs[:, nx:nx + 1]).then_inc(sem("exp_made"), 1)

            @block.vector
            def _(dve):
                own = Chain(dve, sem("own_d"))
                dve.wait_ge(sem("c_scored"), 1)
                own.link(nc.vector.tensor_reduce(mx, r3(PS[:, 0:NH * P], NH), AX.X, ALU.max))
                nc.vector.tensor_tensor(r3(pr[0][:, 0:NH * P], NH), r3(PS[:, 0:NH * P], NH), bc(mx, P), ALU.subtract).then_inc(sem("c_shifted"), 1)
                dve.wait_ge(sem("c_exp"), 1)
                own.link(nc.vector.tensor_reduce(rs, r3(pr[0][:, 0:NH * P], NH), AX.X, ALU.add))
                own.link(nc.vector.reciprocal(rrs, rs))
                dve.wait_ge(sem("c_mixed"), 1)
                nc.vector.tensor_tensor(r3(oatt[:, 0, :], NH), r3(bank(4), NH), bc(rrs, HD), ALU.mult).then_inc(sem("c_done"), 1)

                own_l = Chain(dve, sem("own_dl"))

                def top(n, hh):
                    wait(dve, sem("scored"), n + 1)
                    own_l.link(nc.vector.tensor_reduce(mx[:, hh:hh + 1], PS[:, (hh % 2) * 3 * H:(hh % 2) * 3 * H + KEYS], AX.X, ALU.max))
                    nc.vector.tensor_scalar(nmx[:, hh:hh + 1], mx[:, hh:hh + 1], -SCALE, None, ALU.mult).then_inc(sem("max_made"), 1)

                top(0, 0)
                with dve.Fori(0, NS) as t:
                    own_l.start(t * 2 * NH + 1)

                    def finish(n, hh):
                        wait(dve, sem("mixed"), n + 1)
                        own_l.link(nc.vector.reciprocal(rrs[:, hh:hh + 1], rs[:, hh:hh + 1]))
                        nc.vector.tensor_scalar(oatt[:, ds(t + 1, 1), hh * HD:(hh + 1) * HD], bank(7, HD, hh % RG * P + head(hh)[0] * HD).unsqueeze(1),
                                                rrs[:, hh:hh + 1], None, ALU.mult).then_inc(sem("head_done"), 1)

                    for hh in range(NH):
                        n = t * NH + hh
                        top(n + 1, (hh + 1) % NH)
                        if hh >= 1:
                            finish(n - 1, hh - 1)
                        wait(dve, sem("p_transposed"), n * 3 + 2)
                        nc.vector.tensor_copy(pT[hh % 2][:, H:2 * H], bank(6)).then_inc(sem("pT_rest"), 1)
                        wait(dve, sem("p_transposed"), n * 3 + 3)
                        nc.vector.tensor_copy(pT[hh % 2][:, 2 * H:KEYS], bank(6, 2 * P)).then_inc(sem("pT_rest"), 1)
                    finish(n, NH - 1)

            @block.tensor
            def _(pe):
                pe.wait_ge(sem("cache_in"), 16 * 2 * NC)
                for a in range(NC):
                    last = nc.tensor.transpose(bank(7, P, a * P), kc[:, a, :], ident)
                last.then_inc(sem("kcT_made"), 1)
                for hh in range(NH):
                    v, r = head(hh)
                    rows = slice(HD * v, HD * v + HD)
                    last = nc.tensor.matmul(PS[:, hh * P:(hh + 1) * P], qaT[rows, r, 0:P], kaT[rows, 0:P], start=True, stop=True)
                last.then_inc(sem("c_scored"), 1)
                pe.wait_ge(sem("c_exp"), 1)
                for hh in range(NH):
                    last = nc.tensor.transpose(PS[:, 2 * H + hh * P:2 * H + (hh + 1) * P], pr[0][:, hh * P:(hh + 1) * P], ident)
                last.then_inc(sem("c_transposed"), 1)
                pe.wait_ge(sem("c_pT"), 1)
                for hh in range(NH):
                    v, r = head(hh)
                    last = nc.tensor.matmul(bank(4, HD, hh * HD), pT[0][:, hh * P:(hh + 1) * P], va[:, 0, v * HD:(v + 1) * HD], start=True, stop=True)
                last.then_inc(sem("c_mixed"), 1)
                pe.wait_ge(sem("c_done"), 1)
                pe.wait_ge(sem("kcT_kept"), 1)

                def score(a, hh, tile):
                    v, r = head(hh)
                    rows = slice(HD * v, HD * v + HD)
                    if a == 0 and v == 0:
                        wait(pe, sem("q_staged"), tile * RG + (r + 1))
                    w = min(H, KEYS - a * H)
                    last = nc.tensor.matmul(bank((hh % 2) * 3 + a, w), qst[rows, r * P:(r + 1) * P],
                                            kaT[rows, P + a * H:P + a * H + w], start=True, stop=True)
                    if a == 2:
                        last.then_inc(sem("scored"), 1)

                for hh in range(AHEAD):
                    for a in range(3):
                        score(a, hh, 0)
                with pe.Fori(0, NS) as t:
                    for hh in range(NH):
                        n = t * NH + hh
                        v = head(hh)[0]
                        later = ((hh + AHEAD) % NH, t + (hh + AHEAD) // NH)

                        def turn(k0, k1):
                            for k in range(k0, k1):
                                last = nc.tensor.transpose(bank(6, P, (k - k0) * P), pr[hh % 2][:, k * P:(k + 1) * P], ident)
                            last.then_inc(sem("p_transposed"), 1)

                        wait(pe, sem("exp_made"), n + 1)
                        wait(pe, sem("pT_rest"), n * 2)
                        turn(0, 4)
                        score(0, *later)
                        wait(pe, sem("pT_first"), n + 1)
                        turn(4, 8)
                        score(1, *later)
                        wait(pe, sem("pT_rest"), n * 2 + 1)
                        turn(8, NS + NC)
                        score(2, *later)
                        for k in range(NS + NC):
                            if k == 8:
                                wait(pe, sem("pT_rest"), n * 2 + 2)
                            last = nc.tensor.matmul(bank(7, P, hh % RG * P), pT[hh % 2][:, k * P:(k + 1) * P], va[:, 1 + k, :], start=(k == 0), stop=(k == NS + NC - 1))
                        last.then_inc(sem("mixed"), 1)

        w_gu_v = t_in["w_gu"][0].rearrange("e (j p) n -> e p j n", p=P)
        w_dn_v = t_in["w_down"][0].rearrange("e (j p) n -> e p j n", p=P)

        def chunk_src(e, c):
            if c < 4:
                lo = (c % 2) * FF + (c // 2) * H
                return w_gu_v[ds(e, 1), :, :, lo:lo + H].rearrange("o p j n -> (o p) j n")
            j0 = (c - 4) * KT // 2
            return w_dn_v[ds(e, 1), :, j0:j0 + KT // 2, :].rearrange("o p j n -> (o p) j n")

        def rows_of(ap, c):
            return r3(ap, KT if c < 4 else KT // 2)

        def slot_of(c):
            return c if c < RAW_SLOTS else c - 3

        def raw_chunk(c):
            return rows_of(raw[slot_of(c)], c)

        with stage("w_in0 w_in1 w_in2") as block:
            @block.sync
            def _(sp):
                sp.dma_start(w_rt, w_rt_v).then_inc(sem("w_rt_in"), 16)

                def tile(g, x_src):
                    wait(sp, sem("x1_made"), g)
                    sp.dma_start(xr, x_src).then_inc(sem("xr_in"), 16)
                    wait(sp, sem("x1_made"), g + 1)
                    sp.dma_start(x1_d[ds(g * P, P), :], x1).then_inc(sem("x1_out"), 16)
                    wait(sp, sem("h2_made"), g + 1)
                    sp.dma_start(h2_d[ds(g * P, P), :], h2).then_inc(sem("h2_out"), 16)

                tile(0, x_ctx)
                with sp.Fori(1, NT) as g:
                    tile(g, x_lat[ds(g * P - P, P), :])
                sp.wait_ge(sem("x1_out"), 16 * NT)
                sp.wait_ge(sem("h2_out"), 16 * NT)
                sp.wait_ge(sem("zeros_out"), 16 * (NT + 2))

            @block.scalar
            def _(act):
                for c in range(RAW_SLOTS - 1):
                    act.dma_start(raw_chunk(c), chunk_src(0, c)).then_inc(sem(f"w_in{c}"), 16)
                act.wait_ge(sem("zeroed"), 1)
                for a in range(NT + 1):
                    act.dma_start(moe_d[a * P:(a + 1) * P, :], zeros).then_inc(sem("zeros_out"), 16)
                act.dma_start(h2_d[TOK:TOK + PADS, :], zeros).then_inc(sem("zeros_out"), 16)

                def turned_mix(g):
                    wait(act, sem("mix_transposed"), g + 1)
                    wait(act, sem("projected"), g)
                    nc.scalar.activation(mixT, PS[:, 2 * H:4 * H], ACT.Copy).then_inc(sem("mixT_made"), 1)

                def square(g):
                    wait(act, sem("x1_made"), g + 1)
                    nc.scalar.activation(junkE, x1, ACT.Square, accum_out=ss).then_inc(sem("x1_squared"), 1)

                def turned_h2(b):
                    wait(act, sem("h2_transposed"), b + 1)
                    wait(act, sem("routed"), b)
                    nc.scalar.activation(h2T, PS[:, 4 * H:6 * H], ACT.Copy).then_inc(sem("h2T_made"), 1)

                def gates_exp(b):
                    wait(act, sem("top_made"), b + 1)
                    nc.scalar.activation(exg, top8[:, 0:TOPK], ACT.Exp, bias=ntop, accum_out=gsum).then_inc(sem("gates_exp"), 1)

                turned_mix(0)
                turned_mix(1)
                square(0)
                with act.Fori(1, NT) as g:
                    turned_h2(g - 1)
                    turned_mix(g + 1)
                    gates_exp(g - 1)
                    square(g)
                turned_h2(NT - 1)
                gates_exp(NT - 1)

            @block.gpsimd
            def _(pool):
                nc.gpsimd.memset(zeros, 0.0).then_inc(sem("zeroed"), 1)
                pool.wait_ge(sem("pads_out"), 16)

                def stage_mix(g):
                    wait(pool, sem("mix_transposed"), g)
                    nc.gpsimd.tensor_copy(mixs[:, 0:H], ga_all[:, ds(g, 1), :].rearrange("p o c -> p (o c)"))
                    nc.gpsimd.tensor_copy(mixs[:, H:2 * H], oatt[:, ds(g, 1), :].rearrange("p o c -> p (o c)")).then_inc(sem("mix_staged"), 1)

                def norm(g):
                    wait(pool, sem("x1_mean"), g + 1)
                    nc.gpsimd.tensor_tensor(rstd, msq, negh[:, 0:1], ALU.pow).then_inc(sem("x1_rstd"), 1)

                def scatter(b):
                    wait(pool, sem("entries_made"), b + 1)
                    settle(pool, "pool_steps")
                    for k in range(TOPK):
                        pool.indirect_dma_start(out=list_d, out_offset=bass.IndirectOffsetOnAxis(ap=sloti[:, k:k + 1].bitcast(U32), axis=0),
                                                in_=ent[:, 2 * k:2 * k + 2], in_offset=None).then_inc(sem("listed_out"), 16)

                stage_mix(0)
                stage_mix(1)
                norm(0)
                with pool.Fori(1, NT - 1) as g:
                    stage_mix(g + 1)
                    norm(g)
                    scatter(g - 1)
                pool.wait_ge(sem("mix_transposed"), NT)
                pool.sem_inc(sem("mix_staged"), 1)
                norm(NT - 1)
                scatter(NT - 2)
                scatter(NT - 1)
                pool.wait_ge(sem("listed_out"), 16 * TOPK * NT)

            @block.vector
            def _(dve):
                own = Chain(dve, sem("own_e"))
                FRONT_LINKS, BACK_LINKS = 1, 12
                def front(g, latent):
                    gate = mE[0 if latent else 1][0]
                    wait(dve, sem("projected"), g + 1)
                    wait(dve, sem("x1_out"), g * 16)
                    nc.vector.tensor_tensor(x1, PS[:, 0:DM], gate, ALU.mult).then_inc(sem("mix_gated"), 1)
                    wait(dve, sem("mix_gated"), g + 1)
                    wait(dve, sem("xr_in"), g * 16 + 16)
                    nc.vector.tensor_tensor(x1, x1, xr, ALU.add).then_inc(sem("x1_made"), 1)

                def norm(g, latent):
                    _, scale, shift = mE[0 if latent else 1]
                    wait(dve, sem("x1_squared"), g + 1)
                    nc.vector.tensor_scalar(msq, ss, 1.0 / DM, EPS, ALU.mult, ALU.add).then_inc(sem("x1_mean"), 1)
                    wait(dve, sem("x1_rstd"), g + 1)
                    wait(dve, sem("h2_out"), g * 16)
                    wait(dve, sem("h2_transposed"), g)
                    own.link(nc.vector.scalar_tensor_tensor(h2, x1, rstd, scale, ALU.mult, ALU.mult))
                    nc.vector.tensor_tensor(h2, h2, shift, ALU.add).then_inc(sem("h2_made"), 1)

                def pick(b):
                    wait(dve, sem("routed"), b + 1)
                    own.link(nc.vector.tensor_tensor(logit, bank(6, NE), brt, ALU.add))
                    settle(dve, "dve_steps")
                    own.link(nc.vector.max(out=top8, in_=logit))
                    settle(dve, "dve_steps")
                    own.link(nc.vector.max_index(out=top8i, in_max=top8, in_values=logit))
                    nc.vector.tensor_scalar(ntop, top8[:, 0:1], -1.0, None, ALU.mult).then_inc(sem("top_made"), 1)
                    own.link(nc.vector.tensor_copy(idxf, top8i))
                    own.link(nc.vector.tensor_scalar(picked, expert, idxf[:, 0:1], None, ALU.is_equal))
                    for k in range(1, TOPK):
                        ins = nc.vector.scalar_tensor_tensor(picked, expert, idxf[:, k:k + 1], picked, ALU.is_equal, ALU.add)
                        if k < TOPK - 1:
                            own.link(ins)
                    ins.then_inc(sem("picked_made"), 1)

                def enter(b):
                    wait(dve, sem("gates_exp"), b + 1)
                    own.link(nc.vector.reciprocal(gcp, gsum))
                    wait(dve, sem("listed_out"), b * 64)
                    own.link(nc.vector.tensor_scalar(gates, exg, gcp, None, ALU.mult))
                    own.link(nc.vector.tensor_copy(ent.bitcast(F32)[:, 1:8:2], gates))
                    nc.vector.tensor_copy(ent[:, 0:8:2], tokid[:, ds(b, 1)].broadcast_to([P, TOPK]))
                    wait(dve, sem("placed"), b + 1)
                    own.link(nc.vector.scalar_tensor_tensor(place, expert, float(LISTW), bank(7, NE), ALU.mult, ALU.add))
                    nc.vector.tensor_tensor(pickedsum, pickedsum, picked, ALU.add)
                    for k in range(TOPK):
                        ins = nc.vector.scalar_tensor_tensor(spares[:, k], expert, idxf[:, k:k + 1], place, ALU.is_equal, ALU.mult,
                                                             accum_out=slotf[:, k:k + 1])
                    own.link(ins)
                    nc.vector.tensor_copy(sloti, slotf).then_inc(sem("entries_made"), 1)

                front(0, False)
                norm(0, False)
                assert own.n == FRONT_LINKS
                with dve.Fori(1, NT) as g:
                    own.start(FRONT_LINKS + (g - 1) * (FRONT_LINKS + BACK_LINKS))
                    pick(g - 1)
                    front(g, True)
                    enter(g - 1)
                    norm(g, True)
                    assert own.n == FRONT_LINKS + BACK_LINKS, own.n
                own.start(FRONT_LINKS + (NT - 1) * (FRONT_LINKS + BACK_LINKS))
                pick(NT - 1)
                enter(NT - 1)
                dve.wait_ge(sem("counted"), 1)
                own.link(nc.vector.tensor_scalar(cnti, bank(6, NE), float(P - 1), None, ALU.add))
                own.link(nc.vector.tensor_scalar(cnti, cnti, 7, None, ALU.arith_shift_right))
                own.link(nc.vector.tensor_scalar(ntl, cnti, 1.0, None, ALU.max))
                own.link(nc.vector.memset(tstart[:, 0:1], 0))
                own.link(nc.vector.tensor_tensor_scan(tstartf, ones[:, 0:NE], ntl, 0.0, ALU.mult, ALU.add))
                nc.vector.tensor_copy(tstart[:, 1:NE + 1], tstartf).then_inc(sem("tiles_known"), 1)
                nc.vector.tensor_scalar(tlast, tstartf, -1.0, None, ALU.add).then_inc(sem("tiles_known"), 1)

            @block.tensor
            def _(pe):
                pe.wait_ge(sem("mE_in"), 16 * 6)
                pe.wait_ge(sem("w_out_in"), 16 * KT)
                pe.wait_ge(sem("w_rt_in"), 16)

                def turn_mix(g):
                    wait(pe, sem("mix_staged"), g + 1)
                    wait(pe, sem("mixT_made"), g)
                    for j in range(KT):
                        last = nc.tensor.transpose(PS[:, 2 * H + j * P:2 * H + (j + 1) * P], mixs[:, j * P:(j + 1) * P], ident)
                    last.then_inc(sem("mix_transposed"), 1)

                def project(g, a):
                    if a == 0:
                        wait(pe, sem("mixT_made"), g + 1)
                        wait(pe, sem("mix_gated"), g)
                    for j in range(KT):
                        last = nc.tensor.matmul(bank(a), mixT[:, j * P:(j + 1) * P], w_out[:, j, a * H:(a + 1) * H],
                                                start=(j == 0), stop=(j == KT - 1))
                    if a == 1:
                        last.then_inc(sem("projected"), 1)

                def turn_h2(b):
                    wait(pe, sem("h2_made"), b + 1)
                    wait(pe, sem("h2T_made"), b)
                    for j in range(KT):
                        last = nc.tensor.transpose(PS[:, 4 * H + j * P:4 * H + (j + 1) * P], h2[:, j * P:(j + 1) * P], ident)
                    last.then_inc(sem("h2_transposed"), 1)

                def route(b):
                    wait(pe, sem("h2T_made"), b + 1)
                    wait(pe, sem("top_made"), b)
                    for j in range(KT):
                        last = nc.tensor.matmul(bank(6, NE), h2T[:, j * P:(j + 1) * P], w_rt[:, j, :], start=(j == 0), stop=(j == KT - 1))
                    last.then_inc(sem("routed"), 1)

                def rank(b):
                    wait(pe, sem("picked_made"), b + 1)
                    wait(pe, sem("entries_made"), b)
                    nc.tensor.matmul(bank(7, NE), upper, picked, start=True, stop=False)
                    nc.tensor.matmul(bank(7, NE), ones, pickedsum, start=False, stop=True).then_inc(sem("placed"), 1)

                turn_mix(0)
                project(0, 0)
                project(0, 1)
                turn_mix(1)
                with pe.Fori(1, NT) as g:
                    project(g, 0)
                    turn_h2(g - 1)
                    project(g, 1)
                    route(g - 1)
                    turn_mix(g + 1)
                    rank(g - 1)
                turn_h2(NT - 1)
                route(NT - 1)
                rank(NT - 1)
                pe.wait_ge(sem("entries_made"), NT)
                nc.tensor.matmul(bank(6, NE), ones, pickedsum, start=True, stop=True).then_inc(sem("counted"), 1)

        def bound(eng, e):
            return eng.value_load(tstart[0:1, ds(e, 1)], min_val=0, max_val=MAX_TILES)

        def expert_tiles(eng, body):
            with eng.Fori(0, NE) as e:
                s, n = bound(eng, e), bound(eng, e + 1)
                with eng.Fori(s, n) as j:
                    body(e, j, s)

        def expert_tiles_dividing(eng, body):
            def between(e, s1, last):
                with eng.If_lt(eng.to_reg(s1), last):
                    with eng.Fori(s1, last) as j:
                        body(e, j, False, None)

            with eng.Fori(0, NE - 1) as e:
                s = bound(eng, e)
                last = eng.value_load(tlast[0:1, ds(e, 1)], min_val=0, max_val=MAX_TILES)
                with eng.If_lt(eng.to_reg(s), last):
                    body(e, s, True, None)
                    between(e, s + 1, last)
                    body(e, last, False, last + 1)
                with eng.If_lt(eng.to_reg(last), s + 1):
                    body(e, s, True, s + 1)
            s, n = bound(eng, NE - 1), bound(eng, NE)
            body(NE - 1, s, True, None)
            between(NE - 1, s + 1, n)

        with stage("") as block:
            @block.sync
            def _(sp):
                def load(e, c):
                    if c in (0, 3):
                        wait(sp, sem(f"lo_made{c}"), e)
                    elif c in (1, 2):
                        wait(sp, sem(f"lo_made{c + 3}"), e)
                    else:
                        wait(sp, sem(f"lo_made{c - 3}"), e + 1)
                    sp.dma_start(raw_chunk(c), chunk_src(e, c)).then_inc(sem(f"w_in{slot_of(c)}"), 16)

                def gate_up_bias(e):
                    sp.dma_start(bias[:, 0:2 * FF], t_in["b_gu"][0, ds(e, 1), :].rearrange("o n -> (o n)").partition_broadcast(P)).then_inc(sem("b_gu_in"), 16)

                def down_bias(e):
                    sp.dma_start(bias[:, 2 * FF:2 * FF + DM], t_in["b_down"][0, ds(e, 1), :].rearrange("o n -> (o n)").partition_broadcast(P)).then_inc(sem("b_dn_in"), 16)

                gate_up_bias(0)
                load(0, 3)
                load(0, 4)
                load(0, 5)
                down_bias(0)
                load(1, 0)
                load(1, 1)

                def chunks_of(e, s, ahead):
                    load(e, 2)
                    load(e, 3)
                    wait(sp, sem("gu_biased"), s * 2)
                    gate_up_bias(e)
                    load(e, 4)
                    load(e, 5)
                    if ahead:
                        load(e + 1, 0)
                        load(e + 1, 1)
                    wait(sp, sem("y_biased"), s)
                    down_bias(e)

                with sp.Fori(1, NE - 1) as e:
                    chunks_of(e, bound(sp, e), True)
                chunks_of(NE - 1, bound(sp, NE - 1), False)

            @block.gpsimd
            def _(pool):
                nc.gpsimd.memset(yo, 0.0).then_inc(sem("y_made"), 1)
                nc.gpsimd.memset(held, 0.0).then_inc(sem("first_set"), 1)
                pool.wait_ge(sem("first_set"), 1)
                nc.gpsimd.tensor_scalar(held.bitcast(I32)[:, 0:1], tokid[:, NT - 1:NT], float(P), None, ALU.add).then_inc(sem("held_made"), 1)

                def add_up(j):
                    wait(pool, sem("added_up"), j * 16)
                    wait(pool, sem("held_made"), j + 1)
                    settle(pool, "pool_steps")
                    nc.gpsimd.tensor_copy(current, held).then_inc(sem("taken"), 1)

                    def send():
                        wait(pool, sem("taken"), j + 1)
                        wait(pool, sem("y_made"), j + 1)
                        settle(pool, "pool_steps")
                        pool.indirect_dma_start(out=moe_d, out_offset=bass.IndirectOffsetOnAxis(ap=current.bitcast(U32)[:, 0:1], axis=0),
                                                in_=yo, in_offset=None, compute_op=ALU.add).then_inc(sem("added_up"), 16)
                    return send

                def gather(j):
                    wait(pool, sem("x_turned"), j * 2)
                    settle(pool, "pool_steps")
                    pool.indirect_dma_start(out=xg, out_offset=None, in_=h2_d,
                                            in_offset=bass.IndirectOffsetOnAxis(ap=listed.bitcast(U32)[:, 0:1], axis=0)).then_inc(sem("gathered"), 16)

                def body(e, j, s):
                    wait(pool, sem("held_made"), j + 1)
                    wait(pool, sem("gathered"), j * 16)
                    row = nc.s_assert_within(e * LISTW + (j - s) * P, 0, (NE - 1) * LISTW + TOK - P,
                                             skip_runtime_bounds_check_because="an expert has at most TOK rows, in TOK / 128 tiles")
                    pool.dma_start(listed, list_d[ds(row, P), :]).then_inc(sem("listed_in"), 16)
                    wait(pool, sem("listed_in"), j * 16 + 16)
                    gather(j)
                    send = add_up(j)
                    wait(pool, sem("taken"), j + 1)
                    settle(pool, "pool_steps")
                    nc.gpsimd.tensor_copy(held, listed.bitcast(F32)).then_inc(sem("held_made"), 1)
                    send()

                expert_tiles(pool, body)
                T = pool.value_load(tstart[0:1, NE:NE + 1], min_val=0, max_val=MAX_TILES)
                gather(T)
                add_up(T)()
                wait(pool, sem("added_up"), T * 16 + 16)
                wait(pool, sem("gathered"), T * 16 + 16)

            @block.scalar
            def _(act):
                def hi(e, c, n):
                    if n is not None:
                        wait(act, sem(f"used{c}"), n)
                    loads = 16 * (e + 1) if c in (0, 3) else 32 * e + 16 * (c // RAW_SLOTS + 1)
                    wait(act, sem(f"w_in{slot_of(c)}"), loads)
                    nc.scalar.activation(w_hi[c], raw[slot_of(c)], ACT.Copy).then_inc(sem(f"hi_made{c}"), 1)

                def turned_x(j, half):
                    wait(act, sem("x_turned"), j * 2 + half + 1)
                    nc.scalar.activation(xT_hi[:, half * H:(half + 1) * H], bank(7), ACT.Copy).then_inc(sem("xhi_made"), 1)

                def turned_act(j, half):
                    wait(act, sem("act_turned"), j * 2 + half + 1)
                    nc.scalar.activation(aT_hi[:, half * H:(half + 1) * H], bank(6), ACT.Copy).then_inc(sem("ahi_made"), 1)

                def sigmoid(j, half):
                    wait(act, sem("g_made"), j * 2 + half + 1)
                    wait(act, sem("act_made"), j * 2 + half)
                    nc.scalar.activation(sgm, gw[:, half * H:(half + 1) * H], ACT.Sigmoid, scale=1.702).then_inc(sem("sig_made"), 1)

                turned_x(0, 0)
                turned_x(0, 1)
                for c in range(HI_AHEAD):
                    hi(0, c, None)

                def body(e, j, first, n):
                    def at_last(c):
                        if n is not None:
                            hi(e + 1, c, n)

                    def at_first(c):
                        if first:
                            hi(e, c, j)

                    sigmoid(j, 0)
                    if first:
                        at_first(4)
                    else:
                        at_last(0)
                    turned_act(j, 0)
                    sigmoid(j, 1)
                    if first:
                        at_first(5)
                    else:
                        at_last(1)
                    turned_x(j + 1, 0)
                    turned_act(j, 1)
                    if first:
                        at_last(0)
                    turned_x(j + 1, 1)
                    if first:
                        at_last(1)
                    else:
                        at_last(2)
                    wait(act, sem("y_biased"), j + 1)
                    wait(act, sem("taken"), j + 2)
                    nc.scalar.activation(yo, yo, ACT.Copy, scale=current[:, 1:2]).then_inc(sem("y_made"), 1)
                    if first:
                        at_last(2)
                    at_last(3)

                expert_tiles_dividing(act, body)

            @block.vector
            def _(dve):
                own = Chain(dve, sem("own_f"))
                LINKS = 6

                def lo(e, c, pieces=(0, 1)):
                    n = w_lo[c].shape[1] // 2
                    cols = slice(pieces[0] * n, (pieces[-1] + 1) * n)
                    wait(dve, sem(f"hi_made{c}"), e + 1)
                    ins = nc.vector.tensor_tensor(w_lo[c][:, cols], raw[slot_of(c)][:, cols], w_hi[c][:, cols], ALU.subtract)
                    if pieces[-1] == 1:
                        ins.then_inc(sem(f"lo_made{c}"), 1)

                def x_lo(j, half):
                    cols = slice(half * H, (half + 1) * H)
                    wait(dve, sem("xhi_made"), j * 2 + half + 1)
                    nc.vector.tensor_tensor(xT_lo[:, cols], bank(7), xT_hi[:, cols], ALU.subtract).then_inc(sem("xlo_made"), 1)

                def act_lo(j, half):
                    cols = slice(half * H, (half + 1) * H)
                    wait(dve, sem("ahi_made"), j * 2 + half + 1)
                    nc.vector.tensor_tensor(aT_lo[:, cols], bank(6), aT_hi[:, cols], ALU.subtract).then_inc(sem("alo_made"), 1)

                def gate(e, j, half):
                    g_ = gw[:, half * H:(half + 1) * H]
                    if half == 0:
                        wait(dve, sem("b_gu_in"), e * 16 + 16)
                    wait(dve, sem(f"used{2 * half}"), j + 1)
                    own.link(nc.vector.tensor_tensor(g_, bank(2 * half), bias[:, half * H:(half + 1) * H], ALU.add))
                    nc.vector.tensor_scalar(g_, g_, 7.0, None, ALU.min).then_inc(sem("g_made"), 1)

                def up(j, half):
                    cols = slice(half * H, (half + 1) * H)
                    g_, u_ = gw[:, cols], uw[:, cols]
                    wait(dve, sem(f"used{2 * half + 1}"), j + 1)
                    nc.vector.tensor_tensor(u_, bank(2 * half + 1), bias[:, FF + half * H:FF + (half + 1) * H], ALU.add).then_inc(sem("gu_biased"), 1)
                    wait(dve, sem("gu_biased"), j * 2 + half + 1)
                    own.link(nc.vector.tensor_scalar(u_, u_, 7.0, -7.0, ALU.min, ALU.max))
                    own.link(nc.vector.scalar_tensor_tensor(u_, u_, 1.0, g_, ALU.add, ALU.mult))
                    wait(dve, sem("sig_made"), j * 2 + half + 1)
                    nc.vector.tensor_tensor(act[:, cols], u_, sgm, ALU.mult).then_inc(sem("act_made"), 1)

                x_lo(0, 0)
                x_lo(0, 1)
                for c in range(LO_AHEAD):
                    lo(0, c)

                def body(e, j, first, n):
                    def at_last(c):
                        if n is not None:
                            lo(e + 1, c)

                    def at_first(c, pieces=(0, 1)):
                        if first:
                            lo(e, c, pieces)

                    own.start(j * LINKS)
                    gate(e, j, 0)
                    at_first(3)
                    up(j, 0)
                    at_first(4, (0,))
                    if not first:
                        at_last(0)
                    gate(e, j, 1)
                    act_lo(j, 0)
                    at_first(4, (1,))
                    up(j, 1)
                    x_lo(j + 1, 0)
                    at_first(5, (0,))
                    act_lo(j, 1)
                    at_first(5, (1,))
                    if first:
                        at_last(0)
                    x_lo(j + 1, 1)
                    at_last(1)
                    wait(dve, sem("b_dn_in"), e * 16 + 16)
                    wait(dve, sem("used5"), j + 1)
                    wait(dve, sem("added_up"), j * 16 + 16)
                    nc.vector.tensor_tensor(yo, PS[:, 4 * H:6 * H], bias[:, 2 * FF:2 * FF + DM], ALU.add).then_inc(sem("y_biased"), 1)
                    at_last(2)
                    assert own.n == LINKS

                expert_tiles_dividing(dve, body)

            @block.tensor
            def _(pe):
                def turn_x(j, half):
                    if half == 0:
                        wait(pe, sem("gathered"), j * 16 + 16)
                    wait(pe, sem("xlo_made"), j * 2 + half)
                    for k in range(4):
                        c = half * 4 + k
                        last = nc.tensor.transpose(bank(7, P, k * P), xg[:, c * P:(c + 1) * P], ident)
                    last.then_inc(sem("x_turned"), 1)

                def turn_act(j, half):
                    wait(pe, sem("act_made"), j * 2 + half + 1)
                    wait(pe, sem("alo_made"), j * 2 + half)
                    for k in range(4):
                        c = half * 4 + k
                        last = nc.tensor.transpose(bank(6, P, k * P), act[:, c * P:(c + 1) * P], ident)
                    last.then_inc(sem("act_turned"), 1)

                def product(to, parts, k, c, kk, cols, first, final):
                    hi_, lo_ = (x[:, k * P:(k + 1) * P] for x in parts)
                    wh, wl = rows_of(w_hi[c], c)[:, kk, cols], rows_of(w_lo[c], c)[:, kk, cols]
                    nc.tensor.matmul(to, hi_, wh, start=first, stop=False)
                    nc.tensor.matmul(to, hi_, wl, start=False, stop=False)
                    return nc.tensor.matmul(to, lo_, wh, start=False, stop=final)

                turn_x(0, 0)
                turn_x(0, 1)

                def body(e, j, s):
                    wait(pe, sem("xlo_made"), j * 2 + 2)
                    for c in range(4):
                        wait(pe, sem(f"lo_made{c}"), e + 1)
                        if c in (0, 2):
                            wait(pe, sem("gu_biased"), j * 2)
                        for k in range(KT):
                            last = product(bank(c), (xT_hi, xT_lo), k, c, k, slice(0, H), k == 0, k == KT - 1)
                        last.then_inc(sem(f"used{c}"), 1)
                        if c == 2:
                            turn_act(j, 0)
                    turn_x(j + 1, 0)
                    wait(pe, sem("y_biased"), j)
                    for half in range(2):
                        wait(pe, sem(f"lo_made{4 + half}"), e + 1)
                        wait(pe, sem("alo_made"), j * 2 + half + 1)
                        for a in range(2):
                            for k in range(4):
                                last = product(bank(4 + a), (aT_hi, aT_lo), half * 4 + k, 4 + half, k, slice(a * H, (a + 1) * H),
                                               half == 0 and k == 0, half == 1 and k == 3)
                            if half == 0 and a == 0:
                                turn_act(j, 1)
                        last.then_inc(sem(f"used{4 + half}"), 1)
                        if half == 0:
                            turn_x(j + 1, 1)

                expert_tiles(pe, body)

        with stage("") as block:
            @block.sync
            def _(sp):
                for c in range(2):
                    sp.dma_start(mG[c], spread(mod_d[c, 5])).then_inc(sem("mG_in"), 16)
                sp.dma_start(fn, spread(t_in["final_norm"])).then_inc(sem("mG_in"), 16)

                def load(g, slot):
                    wait(sp, sem("final_made"), g - 1)
                    sp.dma_start(ys[slot], moe_d[ds(g * P, P), :]).then_inc(sem(f"ys_in{slot}"), 16)
                    sp.dma_start(xf[slot], x1_d[ds(g * P, P), :]).then_inc(sem(f"ys_in{slot}"), 16)

                for g in range(2):
                    sp.dma_start(ys[g], moe_d[g * P:(g + 1) * P, :]).then_inc(sem(f"ys_in{g}"), 16)
                    sp.dma_start(xf[g], x1_d[g * P:(g + 1) * P, :]).then_inc(sem(f"ys_in{g}"), 16)
                with sp.Fori(0, NS // 2 - 1) as i:
                    load(i * 2 + 2, 0)
                    load(i * 2 + 3, 1)
                load(NT - 1, 0)

            @block.scalar
            def _(act):
                def body(g, slot, n):
                    wait(act, sem("final_summed"), g + 1)
                    nc.scalar.activation(ys[slot], xf[slot], ACT.Square, accum_out=ss).then_inc(sem("final_squared"), 1)
                    wait(act, sem("final_made"), g + 1)
                    to = t_out["y_prompt"][0] if n is None else t_out["y_sample"][0, ds(g * P - P, P), :]
                    act.dma_start(to, yf[slot]).then_inc(sem(f"y_out{slot}"), 16)

                body(0, 0, None)
                with act.Fori(0, NS // 2) as i:
                    body(i * 2 + 1, 1, 0)
                    body(i * 2 + 2, 0, 0)
                act.wait_ge(sem("y_out0"), 16 * (NS // 2 + 1))
                act.wait_ge(sem("y_out1"), 16 * (NS // 2))

            @block.gpsimd
            def _(pool):
                with pool.Fori(0, NT) as g:
                    wait(pool, sem("final_mean"), g + 1)
                    nc.gpsimd.tensor_tensor(rstd, msq, negh[:, 0:1], ALU.pow).then_inc(sem("final_rstd"), 1)

            @block.vector
            def _(dve):
                own = Chain(dve, sem("own_g"))
                dve.wait_ge(sem("mG_in"), 48)

                def body(g, slot, n, cond):
                    own.start(g)
                    wait(dve, sem(f"ys_in{slot}"), n * 32)
                    own.link(nc.vector.tensor_tensor(ys[slot], ys[slot], mG[cond], ALU.mult))
                    nc.vector.tensor_tensor(xf[slot], xf[slot], ys[slot], ALU.add).then_inc(sem("final_summed"), 1)
                    wait(dve, sem("final_squared"), g + 1)
                    nc.vector.tensor_scalar(msq, ss, 1.0 / DM, EPS, ALU.mult, ALU.add).then_inc(sem("final_mean"), 1)
                    wait(dve, sem("final_rstd"), g + 1)
                    wait(dve, sem(f"y_out{slot}"), n * 16 - 16)
                    nc.vector.scalar_tensor_tensor(yf[slot], xf[slot], rstd, fn, ALU.mult, ALU.mult).then_inc(sem("final_made"), 1)

                body(0, 0, 1, 1)
                with dve.Fori(0, NS // 2) as i:
                    body(i * 2 + 1, 1, i + 1, 0)
                    body(i * 2 + 2, 0, i + 2, 0)


def constants(NS, NT, NE, LISTW, HD, grid_w=64, theta=10000.0):
    import numpy as np

    out = {"ident": np.eye(P, dtype=np.float32)}
    col, row = np.arange(P)[None, :], np.arange(P)[:, None]
    out["upper"] = (col > row).astype(np.float32)
    see = np.stack([np.stack([row <= col] * 2, 1), np.stack([row >= col] * 2, 1)], 1)
    out["seen"] = see.astype(np.int32).reshape(P, 4 * P)
    out["keep"] = (np.arange(NT * P) % P != 0).astype(np.float32)
    out["tokid"] = (row + P * np.arange(NT)[None, :]).astype(np.float32)
    out["expert_id"] = np.arange(NE, dtype=np.float32)
    pads = np.zeros((NE * LISTW, 2), np.int32)
    pads[:, 0] = NT * P + np.arange(NE * LISTW) % P
    out["list_pads"] = pads
    t = np.arange(NS * P)
    inv = (1.0 / (theta ** (np.arange(HD // 4, dtype=np.float32) / np.float32(HD // 4)))).astype(np.float32)
    ang = np.concatenate([(t // grid_w)[:, None].astype(np.float32) * inv, (t % grid_w)[:, None].astype(np.float32) * inv], 1)
    cos, sin = np.cos(ang).astype(np.float32), np.sin(ang).astype(np.float32)
    out["rope"] = np.concatenate([np.repeat(cos, 2, 1), np.stack([-sin, sin], 2).reshape(NS * P, HD)], 1).astype(np.float32)
    return {k: np.ascontiguousarray(v) for k, v in out.items()}


_INS = ["x_prompt", "x_sample", "c", "cache_k", "cache_v", "state_gla_fwd", "state_gla_bwd", "c_ctx", "w_ada", "b_ada",
        "norm_mix", "w_in", "w_gate_f", "b_gate_f", "w_gate_b", "b_gate_b", "gla_norm", "q_norm", "k_norm", "w_out",
        "norm_ffn", "w_router", "b_router", "w_gu", "b_gu", "w_down", "b_down", "final_norm"]
_OUTS = [("y_prompt", (1, 128, 1024)), ("y_sample", (1, 1024, 1024)), ("new_k", (1, 1, 128, 2, 64)),
         ("new_v", (1, 1, 128, 2, 64)), ("new_sf", (1, 1, 4, 64, 128)), ("new_sb", (1, 1, 4, 64, 128))]


def kernel(**inputs):
    import numpy as np
    import concourse.bacc as bacc
    from concourse.bass_utils import run_bass_kernel_spmd

    nc = bacc.Bacc("TRN2", target_bir_lowering=False, num_devices=1)
    arrays = {n: np.ascontiguousarray(inputs[n]) for n in _INS}
    arrays.update(constants(8, 9, 32, 1152, 64))
    t_in, t_out, given = {}, {}, {}
    for n, a in arrays.items():
        given[f"in_{n}"] = a
        t_in[n] = nc.dram_tensor(f"in_{n}", a.shape, mybir.dt.from_np(a.dtype), kind="ExternalInput").ap()
    for n, shape in _OUTS:
        t_out[n] = nc.dram_tensor(f"out_{n}", shape, mybir.dt.float32, kind="ExternalOutput").ap()
    trunk_kernel(nc, t_in, t_out)
    r = run_bass_kernel_spmd(nc, [given], core_ids=[0])
    return tuple(r.results[0][f"out_{n}"] for n, _ in _OUTS)
```
